# Optimizing a Trainium2 kernel written in Bass

```python
import jax, jax.numpy as jnp
from jax import lax
import numpy as np

D_MODEL = 1024
BATCH = 1
SEQ = 256
DEPTH = 2

GRID_W = 64
CTX_LEN = 256
N_HEADS = 16
HEAD_DIM = D_MODEL // N_HEADS
NA_ROWS = 8
NA_COLS = 16
CONV_WIDTH = 3
FFN_HIDDEN = -(-8 * D_MODEL // (3 * 256)) * 256
EPS = 1e-6
NEG_INF = -1e30


def _rms_norm(x, g):
    xf = x.astype(jnp.float32)
    y = xf * lax.rsqrt(jnp.mean(xf * xf, axis=-1, keepdims=True) + EPS)
    return (y * g.astype(jnp.float32)).astype(x.dtype)

def _modulate(h, shift, scale):
    return h * (1 + scale) + shift

def _swiglu(h, w_in, w_out):
    gate, up = jnp.split(h @ w_in, 2, axis=-1)
    return (jax.nn.silu(gate) * up) @ w_out

def _short_conv_mixer(h, w_in, conv_w, w_out):
    b_gate, c_gate, u = jnp.split(h @ w_in, 3, axis=-1)
    z = c_gate * u
    n = z.shape[1]
    pad = CONV_WIDTH // 2
    zp = jnp.pad(z, ((0, 0), (pad, pad), (0, 0)))
    zc = sum(conv_w[j] * zp[:, j:j + n] for j in range(CONV_WIDTH))
    return (b_gate * zc) @ w_out

def _qkv_heads(h, w_qkv, g_q, g_k):
    q, k, v = jnp.split(h @ w_qkv, 3, axis=-1)
    shp = h.shape[:-1] + (N_HEADS, HEAD_DIM)
    return _rms_norm(q.reshape(shp), g_q), _rms_norm(k.reshape(shp), g_k), v.reshape(shp)

def _neighbourhood_attention(h, hc, w_qkv, g_q, g_k, rpb, w_out, with_ctx_out):
    bsz, n, _ = h.shape
    rows = n // GRID_W
    kh = min(NA_ROWS, rows)
    scale = HEAD_DIM ** -0.5
    q, k, v = _qkv_heads(h, w_qkv, g_q, g_k)
    qc, kc, vc = _qkv_heads(hc, w_qkv, g_q, g_k)
    q_g = q.reshape(bsz, rows, GRID_W, N_HEADS, HEAD_DIM)
    k_g = k.reshape(bsz, rows, GRID_W, N_HEADS, HEAD_DIM)
    v_g = v.reshape(bsz, rows, GRID_W, N_HEADS, HEAD_DIM)

    col = jnp.arange(GRID_W)
    col_start = jnp.clip(col - NA_COLS // 2, 0, GRID_W - NA_COLS)
    col_ok = (col[None, :] >= col_start[:, None]) & (col[None, :] < col_start[:, None] + NA_COLS)
    dc = jnp.clip(col[None, :] - col[:, None] + NA_COLS - 1, 0, 2 * NA_COLS - 2)

    def row_block(r):
        r_start = jnp.clip(r - kh // 2, 0, rows - kh)
        q_r = lax.dynamic_index_in_dim(q_g, r, axis=1, keepdims=False)
        k_r = lax.dynamic_slice_in_dim(k_g, r_start, kh, axis=1)
        v_r = lax.dynamic_slice_in_dim(v_g, r_start, kh, axis=1)
        dr = r_start + jnp.arange(kh) - r + NA_ROWS - 1
        bias = rpb[:, dr][:, :, dc].astype(jnp.float32)
        bias = jnp.where(col_ok[None, None], bias, NEG_INF).transpose(0, 2, 1, 3)
        s_win = jnp.einsum('bqhd,brkhd->bhqrk', q_r, k_r,
                           preferred_element_type=jnp.float32) * scale + bias[None]
        s_ctx = jnp.einsum('bqhd,bchd->bhqc', q_r, kc,
                           preferred_element_type=jnp.float32) * scale
        s = jnp.concatenate([s_win.reshape(bsz, N_HEADS, GRID_W, kh * GRID_W), s_ctx], axis=-1)
        p = jax.nn.softmax(s, axis=-1).astype(v.dtype)
        p_win = p[..., :kh * GRID_W].reshape(bsz, N_HEADS, GRID_W, kh, GRID_W)
        p_ctx = p[..., kh * GRID_W:]
        return (jnp.einsum('bhqrk,brkhd->bqhd', p_win, v_r)
                + jnp.einsum('bhqc,bchd->bqhd', p_ctx, vc))

    o = lax.map(row_block, jnp.arange(rows))
    o = jnp.moveaxis(o, 0, 1).reshape(bsz, n, D_MODEL)
    y = o @ w_out
    if not with_ctx_out:
        return y, None
    sc = jnp.einsum('bqhd,bkhd->bhqk', qc, kc, preferred_element_type=jnp.float32) * scale
    pc = jax.nn.softmax(sc, axis=-1).astype(vc.dtype)
    oc = jnp.einsum('bhqk,bkhd->bqhd', pc, vc).reshape(bsz, hc.shape[1], D_MODEL)
    return y, oc @ w_out

def first_inputs(seed: int = 0) -> dict:
    key = jax.random.key(seed)
    ks = jax.random.split(key, 18)
    D = D_MODEL
    n_conv = (DEPTH + 1) // 2
    n_attn = DEPTH // 2

    def nrm(k, shape):
        return jax.random.normal(k, shape, jnp.float32)

    def lin(k, shape, fan_in, gain=1.0):
        return nrm(k, shape) * (gain * fan_in ** -0.5)

    def norm_gain(k, shape):
        return 1.0 + 0.05 * nrm(k, shape)

    return {
        "x": nrm(ks[0], (BATCH, SEQ, D)),
        "c": nrm(ks[1], (BATCH, D)),
        "ctx": nrm(ks[2], (BATCH, CTX_LEN, D)),
        "c_ctx": nrm(ks[3], (D,)),
        "w_ada": lin(ks[4], (DEPTH, D, 6 * D), D, 0.5),
        "b_ada": 0.02 * nrm(ks[5], (DEPTH, 6 * D)),
        "norm_mix": norm_gain(ks[6], (DEPTH, D)),
        "norm_ffn": norm_gain(ks[7], (DEPTH, D)),
        "conv_w_in": lin(ks[8], (n_conv, D, 3 * D), D),
        "conv_w": lin(ks[9], (n_conv, CONV_WIDTH, D), CONV_WIDTH),
        "conv_w_out": lin(ks[10], (n_conv, D, D), D),
        "attn_w_qkv": lin(ks[11], (n_attn, D, 3 * D), D),
        "attn_q_norm": norm_gain(ks[12], (n_attn, HEAD_DIM)),
        "attn_k_norm": norm_gain(ks[13], (n_attn, HEAD_DIM)),
        "attn_rpb": 0.02 * nrm(ks[14], (n_attn, N_HEADS, 2 * NA_ROWS - 1, 2 * NA_COLS - 1)),
        "attn_w_out": lin(ks[15], (n_attn, D, D), D),
        "ffn_w_in": lin(ks[16], (DEPTH, D, 2 * FFN_HIDDEN), D),
        "ffn_w_out": lin(ks[17], (DEPTH, FFN_HIDDEN, D), FFN_HIDDEN),
    }

def first_block(x, c, ctx, c_ctx, w_ada, b_ada, norm_mix, norm_ffn,
              conv_w_in, conv_w, conv_w_out,
              attn_w_qkv, attn_q_norm, attn_k_norm, attn_rpb, attn_w_out,
              ffn_w_in, ffn_w_out):
    for i in range(DEPTH):
        update_ctx = i < DEPTH - 1
        j = i // 2
        mod = jax.nn.silu(c) @ w_ada[i] + b_ada[i]
        mod_c = jax.nn.silu(c_ctx) @ w_ada[i] + b_ada[i]
        sh1, sc1, g1, sh2, sc2, g2 = jnp.split(mod[:, None, :], 6, axis=-1)
        sh1c, sc1c, g1c, sh2c, sc2c, g2c = jnp.split(mod_c, 6, axis=-1)

        h = _modulate(_rms_norm(x, norm_mix[i]), sh1, sc1)
        hc = _modulate(_rms_norm(ctx, norm_mix[i]), sh1c, sc1c)
        if i % 2 == 0:
            y = _short_conv_mixer(h, conv_w_in[j], conv_w[j], conv_w_out[j])
            yc = _short_conv_mixer(hc, conv_w_in[j], conv_w[j], conv_w_out[j]) if update_ctx else None
        else:
            y, yc = _neighbourhood_attention(h, hc, attn_w_qkv[j], attn_q_norm[j], attn_k_norm[j],
                                             attn_rpb[j], attn_w_out[j], update_ctx)
        x = x + g1 * y
        x = x + g2 * _swiglu(_modulate(_rms_norm(x, norm_ffn[i]), sh2, sc2), ffn_w_in[i], ffn_w_out[i])
        if update_ctx:
            ctx = ctx + g1c * yc
            ctx = ctx + g2c * _swiglu(_modulate(_rms_norm(ctx, norm_ffn[i]), sh2c, sc2c),
                                      ffn_w_in[i], ffn_w_out[i])
    return x


DEPTH_2 = 1

N_ATTN_HEADS = 8
ATTN_HEAD_DIM = 64
KV_LATENT = 256
N_IDX_HEADS = 8
IDX_HEAD_DIM = 32
TOPK_MAX = 256
Q_BLOCK = 128
N_RWKV_HEADS = 8
RWKV_HEAD_DIM = 64
DECAY_LORA = 64
AAA_LORA = 64
GATE_LORA = 160
N_GROUPS = 4
EXPERTS_PER_GROUP = 8
N_EXPERTS = N_GROUPS * EXPERTS_PER_GROUP
D_EXPERT = 512
TOP_K_EXPERTS = 2
NORM_EPS = 1e-6
GN_EPS = 64e-5
ATTN_W = N_ATTN_HEADS * ATTN_HEAD_DIM
RWKV_W = N_RWKV_HEADS * RWKV_HEAD_DIM
IDX_Q_W = N_IDX_HEADS * IDX_HEAD_DIM
SHIFT_W = 3 * RWKV_W + DECAY_LORA + AAA_LORA + GATE_LORA
IN_SPLITS = (ATTN_W, KV_LATENT, IDX_Q_W, IDX_HEAD_DIM, N_IDX_HEADS, SHIFT_W, D_MODEL, D_MODEL)
IN_W = ATTN_W + KV_LATENT + IDX_Q_W + IDX_HEAD_DIM + N_IDX_HEADS + SHIFT_W + 2 * D_MODEL


def _split(x, sizes):
    idx = np.cumsum(sizes)[:-1].tolist()
    return jnp.split(x, idx, axis=-1)

def _rmsnorm(x, g):
    xf = x.astype(jnp.float32)
    y = xf * lax.rsqrt(jnp.mean(xf * xf, axis=-1, keepdims=True) + NORM_EPS)
    return (y * g.astype(jnp.float32)).astype(x.dtype)

def _dsa_attention(q, k, v, q_idx, k_idx, w_idx):
    B, S = q.shape[0], q.shape[1]
    top_k = min(TOPK_MAX, S // 4)
    nb = S // Q_BLOCK
    f32 = jnp.float32
    slopes = 2.0 ** (-8.0 * jnp.arange(1, N_ATTN_HEADS + 1, dtype=f32) / N_ATTN_HEADS)
    key_pos = jnp.arange(S)
    k_idx_f = k_idx.astype(f32)
    idx_scale = (IDX_HEAD_DIM ** -0.5) * (N_IDX_HEADS ** -0.5)

    def blocks(a):
        return jnp.moveaxis(a.reshape((B, nb, Q_BLOCK) + a.shape[2:]), 1, 0)

    def one_block(args):
        qb, qib, wib, start = args
        t = start + jnp.arange(Q_BLOCK)
        dots = jnp.einsum('bthd,bsd->bths', qib.astype(f32), k_idx_f)
        score = jnp.einsum('bths,bth->bts', jax.nn.relu(dots), wib.astype(f32)) * idx_scale
        causal = key_pos[None, :] <= t[:, None]
        score = jnp.where(causal[None], score, -jnp.inf)
        _, sel = lax.top_k(score, top_k)
        k_sel = jax.vmap(lambda kb, ib: kb[ib])(k, sel)
        v_sel = jax.vmap(lambda vb, ib: vb[ib])(v, sel)
        logits = jnp.einsum('bthd,btkhd->bthk', qb.astype(f32), k_sel.astype(f32)) * (ATTN_HEAD_DIM ** -0.5)
        dist = (t[None, :, None] - sel).astype(f32)
        logits = logits - slopes[None, None, :, None] * dist[:, :, None, :]
        valid = sel <= t[None, :, None]
        logits = jnp.where(valid[:, :, None, :], logits, -jnp.inf)
        p = jax.nn.softmax(logits, axis=-1)
        o = jnp.einsum('bthk,btkhd->bthd', p, v_sel.astype(f32))
        return o.astype(q.dtype)

    starts = jnp.arange(nb) * Q_BLOCK
    out = lax.map(one_block, (blocks(q), blocks(q_idx), blocks(w_idx), starts))
    return jnp.moveaxis(out, 0, 1).reshape(B, S, ATTN_W)

def _rwkv7_time_mix(p_shift, mu, w0, w2, a0, a2, g2, k_k, k_a, r_k, ln_w, ln_b):
    B, S = p_shift.shape[0], p_shift.shape[1]
    H, N = N_RWKV_HEADS, RWKV_HEAD_DIM
    f32 = jnp.float32
    prev = jnp.pad(p_shift[:, :-1], ((0, 0), (1, 0), (0, 0)))
    mixed = p_shift + (prev - p_shift) * mu
    r, k, v, wl, al, gl = _split(mixed, (RWKV_W, RWKV_W, RWKV_W, DECAY_LORA, AAA_LORA, GATE_LORA))
    w = -jax.nn.softplus(-(w0 + jnp.tanh(wl) @ w2)) - 0.5
    decay = jnp.exp(-jnp.exp(w.astype(f32)))
    a = jax.nn.sigmoid(a0 + al @ a2)
    g = jax.nn.sigmoid(gl) @ g2
    heads = lambda z: z.reshape(B, S, H, N).astype(f32)
    kk = heads(k * k_k)
    kk = kk / jnp.maximum(jnp.sqrt(jnp.sum(kk * kk, axis=-1, keepdims=True)), 1e-12)
    k = k * (1.0 + (a - 1.0) * k_a)
    r_h, k_h, v_h, a_h, d_h = heads(r), heads(k), heads(v), heads(a), heads(decay)

    def step(state, inp):
        r_t, d_t, k_t, v_t, kk_t, b_t = inp
        sa = jnp.einsum('bhij,bhj->bhi', state, -kk_t)
        state = state * d_t[:, :, None, :] + sa[..., None] * b_t[:, :, None, :] + v_t[..., None] * k_t[:, :, None, :]
        y = jnp.einsum('bhij,bhj->bhi', state, r_t)
        return state, y

    xs = tuple(jnp.moveaxis(z, 1, 0) for z in (r_h, d_h, k_h, v_h, kk, kk * a_h))
    _, y = lax.scan(step, jnp.zeros((B, H, N, N), f32), xs)
    y = jnp.moveaxis(y, 0, 1)
    mean = jnp.mean(y, axis=-1, keepdims=True)
    var = jnp.mean(jnp.square(y - mean), axis=-1, keepdims=True)
    y = ((y - mean) * lax.rsqrt(var + GN_EPS)).reshape(B, S, RWKV_W) * ln_w + ln_b
    bonus = (jnp.sum(r_h * k_h * r_k, axis=-1, keepdims=True) * v_h).reshape(B, S, RWKV_W)
    return ((y + bonus) * g).astype(p_shift.dtype)

def _hier_moe(xt, wg_router, we_router, e_bias, w_gate, w_up, w_down):
    T, D = xt.shape
    f32 = jnp.float32
    p_group = jax.nn.softmax((xt @ wg_router).astype(f32), axis=-1)
    g_sel = jnp.argmax(p_group, axis=-1)
    p_gsel = jnp.max(p_group, axis=-1)
    e_logits = (xt @ we_router).astype(f32).reshape(T, N_GROUPS, EXPERTS_PER_GROUP) + e_bias.astype(f32).reshape(N_GROUPS, EXPERTS_PER_GROUP)
    e_in = jnp.take_along_axis(e_logits, g_sel[:, None, None], axis=1)[:, 0]
    top_v, top_i = lax.top_k(e_in, TOP_K_EXPERTS)
    w_top = jax.nn.softmax(top_v, axis=-1) * p_gsel[:, None]
    expert_id = g_sel[:, None] * EXPERTS_PER_GROUP + top_i
    combine = jnp.sum(jax.nn.one_hot(expert_id, N_EXPERTS, dtype=f32) * w_top[..., None], axis=1)

    def body(acc, ew):
        wg, wu, wd, cw = ew
        hdn = jax.nn.silu(xt @ wg) * (xt @ wu)
        return acc + cw[:, None] * (hdn @ wd).astype(f32), None

    acc, _ = lax.scan(body, jnp.zeros((T, D), f32), (w_gate, w_up, w_down, combine.T))
    return acc.astype(xt.dtype)

def second_inputs(seed: int = 0) -> dict:
    key = jax.random.key(seed)
    ks = iter(jax.random.split(key, 40))
    nrm = lambda shape, scale: jax.random.normal(next(ks), shape, jnp.float32) * scale
    L = DEPTH_2
    return {
        "x": nrm((BATCH, SEQ, D_MODEL), 1.0),
        "c": nrm((BATCH, D_MODEL), 1.0),
        "ada_w": nrm((L, D_MODEL, 6 * D_MODEL), 0.5 * D_MODEL ** -0.5),
        "ada_b": nrm((L, 6 * D_MODEL), 0.02),
        "mix_norm_g": 1.0 + nrm((L, D_MODEL), 0.02),
        "w_in": nrm((L, D_MODEL, IN_W), D_MODEL ** -0.5),
        "kv_norm_g": 1.0 + nrm((L, KV_LATENT), 0.02),
        "w_kv_up": nrm((L, KV_LATENT, 2 * ATTN_W), KV_LATENT ** -0.5),
        "q_norm_g": 1.0 + nrm((L, ATTN_HEAD_DIM), 0.02),
        "k_norm_g": 1.0 + nrm((L, ATTN_HEAD_DIM), 0.02),
        "rwkv_mu": jax.random.uniform(next(ks), (L, SHIFT_W), jnp.float32, 0.2, 0.8),
        "rwkv_w0": -1.0 + nrm((L, RWKV_W), 0.5),
        "rwkv_w2": nrm((L, DECAY_LORA, RWKV_W), 0.5 * DECAY_LORA ** -0.5),
        "rwkv_a0": nrm((L, RWKV_W), 0.1),
        "rwkv_a2": nrm((L, AAA_LORA, RWKV_W), 0.5 * AAA_LORA ** -0.5),
        "rwkv_g2": nrm((L, GATE_LORA, RWKV_W), GATE_LORA ** -0.5),
        "rwkv_k_k": 0.85 + nrm((L, RWKV_W), 0.02),
        "rwkv_k_a": 1.0 + nrm((L, RWKV_W), 0.02),
        "rwkv_r_k": nrm((L, N_RWKV_HEADS, RWKV_HEAD_DIM), 0.1),
        "rwkv_ln_w": 1.0 + nrm((L, RWKV_W), 0.02),
        "rwkv_ln_b": nrm((L, RWKV_W), 0.02),
        "w_branch_attn": nrm((L, ATTN_W, D_MODEL), ATTN_W ** -0.5),
        "w_branch_rwkv": nrm((L, RWKV_W, D_MODEL), RWKV_W ** -0.5),
        "w_out": nrm((L, D_MODEL, D_MODEL), D_MODEL ** -0.5),
        "moe_norm_g": 1.0 + nrm((L, D_MODEL), 0.02),
        "router_group_w": nrm((L, D_MODEL, N_GROUPS), D_MODEL ** -0.5),
        "router_expert_w": nrm((L, D_MODEL, N_EXPERTS), D_MODEL ** -0.5),
        "router_expert_bias": nrm((L, N_EXPERTS), 0.01),
        "expert_w_gate": nrm((L, N_EXPERTS, D_MODEL, D_EXPERT), D_MODEL ** -0.5),
        "expert_w_up": nrm((L, N_EXPERTS, D_MODEL, D_EXPERT), D_MODEL ** -0.5),
        "expert_w_down": nrm((L, N_EXPERTS, D_EXPERT, D_MODEL), D_EXPERT ** -0.5),
    }

def second_block(x, c, ada_w, ada_b, mix_norm_g, w_in, kv_norm_g, w_kv_up, q_norm_g, k_norm_g,
              rwkv_mu, rwkv_w0, rwkv_w2, rwkv_a0, rwkv_a2, rwkv_g2, rwkv_k_k, rwkv_k_a, rwkv_r_k,
              rwkv_ln_w, rwkv_ln_b, w_branch_attn, w_branch_rwkv, w_out, moe_norm_g,
              router_group_w, router_expert_w, router_expert_bias, expert_w_gate, expert_w_up,
              expert_w_down):
    B, S, D = x.shape
    h = x
    for l in range(DEPTH_2):
        mod = jax.nn.silu(c) @ ada_w[l] + ada_b[l]
        sh1, sc1, gt1, sh2, sc2, gt2 = jnp.split(mod[:, None, :], 6, axis=-1)

        xn = _rmsnorm(h, mix_norm_g[l]) * (1.0 + sc1) + sh1
        proj = xn @ w_in[l]
        q_a, kv_lat, q_i, k_i, w_i, p_shift, gate_a, gate_r = _split(proj, IN_SPLITS)
        q = _rmsnorm(q_a.reshape(B, S, N_ATTN_HEADS, ATTN_HEAD_DIM), q_norm_g[l])
        kv = _rmsnorm(kv_lat, kv_norm_g[l]) @ w_kv_up[l]
        k_lin, v_lin = jnp.split(kv, 2, axis=-1)
        k = _rmsnorm(k_lin.reshape(B, S, N_ATTN_HEADS, ATTN_HEAD_DIM), k_norm_g[l])
        v = v_lin.reshape(B, S, N_ATTN_HEADS, ATTN_HEAD_DIM)
        o_attn = _dsa_attention(q, k, v, q_i.reshape(B, S, N_IDX_HEADS, IDX_HEAD_DIM), k_i, w_i)
        o_rwkv = _rwkv7_time_mix(p_shift, rwkv_mu[l], rwkv_w0[l], rwkv_w2[l], rwkv_a0[l], rwkv_a2[l],
                                 rwkv_g2[l], rwkv_k_k[l], rwkv_k_a[l], rwkv_r_k[l], rwkv_ln_w[l], rwkv_ln_b[l])
        merged = jax.nn.sigmoid(gate_a) * (o_attn @ w_branch_attn[l]) + jax.nn.sigmoid(gate_r) * (o_rwkv @ w_branch_rwkv[l])
        h = h + gt1 * (merged @ w_out[l])

        xn2 = _rmsnorm(h, moe_norm_g[l]) * (1.0 + sc2) + sh2
        moe = _hier_moe(xn2.reshape(B * S, D), router_group_w[l], router_expert_w[l], router_expert_bias[l],
                        expert_w_gate[l], expert_w_up[l], expert_w_down[l])
        h = h + gt2 * moe.reshape(B, S, D)
    return h


def setup_inputs(seed=0):
    out = dict(first_inputs(seed))
    for name, value in second_inputs(seed + 1).items():
        if name != "x":
            out[name + "_2"] = value
    return out


def reference(
    x, c, ctx, c_ctx, w_ada, b_ada, norm_mix, norm_ffn, conv_w_in, conv_w, conv_w_out,
    attn_w_qkv, attn_q_norm, attn_k_norm, attn_rpb, attn_w_out, ffn_w_in, ffn_w_out, c_2,
    ada_w_2, ada_b_2, mix_norm_g_2, w_in_2, kv_norm_g_2, w_kv_up_2, q_norm_g_2, k_norm_g_2,
    rwkv_mu_2, rwkv_w0_2, rwkv_w2_2, rwkv_a0_2, rwkv_a2_2, rwkv_g2_2, rwkv_k_k_2, rwkv_k_a_2,
    rwkv_r_k_2, rwkv_ln_w_2, rwkv_ln_b_2, w_branch_attn_2, w_branch_rwkv_2, w_out_2,
    moe_norm_g_2, router_group_w_2, router_expert_w_2, router_expert_bias_2, expert_w_gate_2,
    expert_w_up_2, expert_w_down_2,
):
    x = first_block(
        x, c, ctx, c_ctx, w_ada, b_ada, norm_mix, norm_ffn, conv_w_in, conv_w, conv_w_out,
        attn_w_qkv, attn_q_norm, attn_k_norm, attn_rpb, attn_w_out, ffn_w_in, ffn_w_out,
    )
    return second_block(
        x, c_2, ada_w_2, ada_b_2, mix_norm_g_2, w_in_2, kv_norm_g_2, w_kv_up_2, q_norm_g_2,
        k_norm_g_2, rwkv_mu_2, rwkv_w0_2, rwkv_w2_2, rwkv_a0_2, rwkv_a2_2, rwkv_g2_2,
        rwkv_k_k_2, rwkv_k_a_2, rwkv_r_k_2, rwkv_ln_w_2, rwkv_ln_b_2, w_branch_attn_2,
        w_branch_rwkv_2, w_out_2, moe_norm_g_2, router_group_w_2, router_expert_w_2,
        router_expert_bias_2, expert_w_gate_2, expert_w_up_2, expert_w_down_2,
    )


_drawn_inputs = setup_inputs


def setup_inputs(seed=0):
    import zlib

    import numpy as np

    out = dict(_drawn_inputs(seed))
    spreads = {}
    factors = {'attn_q_norm': 8.0,
     'attn_k_norm': 8.0,
     'attn_rpb': 60.301,
     'mix_norm_g_2': 4.759,
     'kv_norm_g_2': 64.0,
     'q_norm_g_2': 64.0,
     'k_norm_g_2': 64.0,
     'rwkv_w2_2': 52.704,
     'rwkv_a0_2': 8.0,
     'rwkv_a2_2': 3.239,
     'rwkv_k_k_2': 64.0,
     'rwkv_k_a_2': 8.0,
     'rwkv_r_k_2': 2.752,
     'rwkv_ln_w_2': 64.0,
     'rwkv_ln_b_2': 64.0,
     'moe_norm_g_2': 22.905,
     'router_expert_bias_2': 64.0,
     'rwkv_w0_2': 8.0}
    for name, (base, spread) in spreads.items():
        noise = np.random.default_rng([zlib.crc32(name.encode()), seed]).standard_normal(out[name].shape)
        drawn = base * np.exp(spread * noise) if base else spread * noise
        out[name] = __import__('jax').numpy.asarray(drawn.astype(out[name].dtype))
    for name, factor in factors.items():
        out[name] = (out[name] * factor).astype(out[name].dtype)
    return out
```

```python
from contextlib import ExitStack

import numpy as np

import concourse.bass as bass
from concourse import mybir

F32 = mybir.dt.float32
ALU = mybir.AluOpType
ACT = mybir.ActivationFunctionType
AX = mybir.AxisListType

P = 128
D = 1024
KD = D // P
SEQ = 256
FH = 2816
KF = FH // P
EPS = 1e-6
GN_EPS = 64e-5
NEG = -1e30
GRID_W, NA_ROWS, NA_COLS = 64, 8, 16
HEADS1 = 16
HEADS2 = 8
HD = 64
LAT = 256
TOPK = 64
NE = 32
EPG = 8
CH = 64
NCH = SEQ // CH
HP = HEADS2 // 2
RING = 24576

STREAM = [
    ("ada0", 12, 4096, 6, 1),
    ("conv", 8, 3072, 8, 1),
    ("cout", 2, 4096, 6, 4),
    ("fin0", 22, 2048, 11, 1),
    ("fout0", 8, 2816, 4, 1),
    ("ada1", 12, 4096, 6, 1),
    ("qkv", 6, 4096, 6, 4),
    ("aout", 2, 4096, 6, 4),
    ("fin1", 22, 2048, 11, 1),
    ("fout1", 8, 2816, 4, 1),
    ("ada2", 12, 4096, 6, 1),
    ("win", 6, 4096, 6, 4),
    ("kvup", 1, 2048, 1, 1),
    ("lora", 1, 1536, 1, 1),
    ("gates", 8, 3072, 8, 1),
    ("wout", 2, 4096, 6, 4),
    ("moe", 96, 4096, 6, 1),
]


def plan_stream():
    plan, owners, count, shared = {}, [], [0] * 11, {}
    for name, n, size, ring, _ in STREAM:
        first = []
        for s in range(min(n, ring)):
            a, b = s * size, (s + 1) * size
            hit = [o for o in owners if o[0] < b and a < o[1]] + [shared[k] for k in (s,) if k in shared]
            first.append(max(hit, key=lambda o: o[2])[3:] if hit else None)
        plan[name] = dict(n=n, size=size, ring=ring, first=first, base=list(count))
        for s in range(min(n, ring)):
            last = max(i for i in range(n) if i % ring == s)
            a, b = s * size, (s + 1) * size
            owners = [o for o in owners if not (a <= o[0] and o[1] <= b)]
            owners.append((a, b, len(plan) * 1000 + last, name, last))
            shared[s] = owners[-1]
            count[s] += 16 * (last // ring + 1)
    return plan


VECS = [
    ("b_ada", 144), ("g_norm", 48), ("conv_w", 24), ("qk1", 2), ("qk2", 2), ("g_lat", 2),
    ("mu", 15), ("w0", 4), ("a0", 4), ("k_k", 4), ("k_a", 4), ("r_k", 4), ("ln_w", 4), ("ln_b", 4),
    ("cs", 24), ("e_bias", 32), ("w_i", 64), ("router", 288),
]
VOFF, _o = {}, 0
for _n, _w in VECS:
    VOFF[_n] = _o
    _o += _w
NVEC = _o
CONSTS = [("ident", 128), ("ones", 128), ("bo64", 128), ("id64", 64), ("strict", 64), ("incl", 64),
          ("level", 384), ("iota", 32), ("eps", 3)]
COFF, _o = {}, 0
for _n, _w in CONSTS:
    COFF[_n] = _o
    _o += _w
NCONST = _o


def build(nc, xin, vecs, consts, colmask, dist, reset, rpb, W, out):
    plan = plan_stream()
    with ExitStack() as ctx:
        def sb(name, cols):
            return ctx.enter_context(nc.sbuf_tensor(name, [P, cols], F32))

        sems = {}

        def sem(name):
            if name not in sems:
                sems[name] = ctx.enter_context(nc.semaphore(name))
            return sems[name]

        ring = sb("ring", RING)
        X = sb("X", 4096)
        A = sb("A", 20480)
        C = sb("C", NCONST)
        V = sb("V", NVEC)
        MOD = sb("MOD", 3 * 96)
        AB = sb("AB", 6 * 16)
        CS = sb("CS", 24)
        RN = sb("RN", 512)
        CM = sb("CM", 64)[:, :]
        SC = sb("SC", 1344)
        PS = ctx.enter_context(nc.psum_tensor("PS", [P, 8, 512], F32))

        def con(name, a=0, b=None):
            w = dict(CONSTS)[name]
            return C[:, COFF[name] + a:COFF[name] + (w if b is None else b)]

        def vec(name, a=0, b=None):
            w = dict(VECS)[name]
            return V[:, VOFF[name] + a:VOFF[name] + (w if b is None else b)]

        ident, ones, bo64 = con("ident"), con("ones"), con("bo64")
        eps, gn_eps, eps_q = (con("eps", i, i + 1) for i in range(3))

        def slot(stage, s, a, b, p0=0, p1=P):
            o = plan[stage]["size"] * (s % plan[stage]["ring"])
            return ring[p0:p1, o + a:o + b]

        def slot_landed(eng, stage, s, turn=0):
            eng.wait_ge(sem(f"landed{s}"), plan[stage]["base"][s] + 16 * (turn + 1))

        def mod(layer, chunk, cond):
            o = layer * 96 + chunk * 2 + cond
            return MOD[:, o:o + 1]

        def mod2(layer, c0):
            return MOD[:, layer * 96 + 2 * c0:layer * 96 + 2 * (c0 + 8)].rearrange("p (k c) -> p k c", c=2)

        NORMS = [(0, 0, 2, 0), (24, 0, 2, 0), (0, 1, 2, 0), (24, 1, 1, 0), (0, 2, 1, 1), (24, 2, 1, 1)]
        HB = [0]
        for nn in NORMS:
            HB.append(HB[-1] + 8 * nn[2])
        H = A[:, 0:4096]

        RES = [("cout", 16, 0, 2), ("fout0", 40, 0, 2), ("aout", 16, 1, 1), ("fout1", 40, 1, 1),
               ("wout", 16, 2, 1)]
        RB, _r = {}, 0
        for stage, _, _, s2 in RES:
            RB[stage] = _r
            _r += 8 * s2
        RB["end"] = _r

        def h_of(k, T):
            return H[:, k * T:(k + 1) * T]

        HID = A[:, 4096:15360]
        SQ = A[:, 4096:8192]

        YC = A[:, 4096:8192]
        CT = A[:, 8192:9216]
        Z = A[:, 9216:9732].rearrange("p (s t) -> p s t", s=2)
        T1 = A[:, 9732:10244].rearrange("p (s t) -> p s t", s=2)
        Q1 = A[:, 4096:6144].rearrange("p (c t) -> p c t", c=8)
        K1 = A[:, 6144:10240].rearrange("p (c t) -> p c t", c=8)
        V1 = A[:, 10240:14336].rearrange("p (c t) -> p c t", c=4)
        RPB = A[:, 14336:20480]
        P1B = A[:, 0:1024].rearrange("p (b t) -> p b t", b=2)
        PT1 = A[:, 1024:2048].rearrange("p (b t) -> p b t", b=2)
        O1 = A[:, 2048:4096]
        XN = A[:, 0:2048]
        RP = A[:, 2048:5888]
        OA = A[:, 5888:6912]
        LATB = A[:, 6912:7424]
        QA = A[:, 7424:8448].rearrange("p (c t) -> p c t", c=4)
        KA = A[:, 8448:9472].rearrange("p (c t) -> p c t", c=4)
        VA = A[:, 9472:10496].rearrange("p (c t) -> p c t", c=2)
        QI = A[:, 10496:11008].rearrange("p (c t) -> p c t", c=2)
        KI = A[:, 11008:11264]
        SCO = A[:, 11264:11776].rearrange("p (c t) -> p c t", c=2)
        NEGM = A[:, 11776:12288].rearrange("p (c t) -> p c t", c=2)
        SEL = A[:, 12288:12800].rearrange("p (c t) -> p c t", c=2)
        DIST = A[:, 12800:13312].rearrange("p (c t) -> p c t", c=2)
        BI = A[:, 13312:13824].rearrange("p (b t) -> p b t", b=2)
        P2B = A[:, 13824:14336].rearrange("p (b t) -> p b t", b=2)
        PT2 = A[:, 14336:14848].rearrange("p (b t) -> p b t", b=2)
        RL = A[:, 14848:15872].rearrange("p (b t) -> p b t", b=4)
        LSQ = A[:, 15872:16384]
        RR, RK, RV = A[:, 2816:3840], A[:, 3840:4864], A[:, 4864:5888]
        DF = A[:, 6912:10752]
        WW, AA, GG, KK = A[:, 6912:7936], A[:, 7936:8960], A[:, 8960:9984], A[:, 9984:11008]
        TS, RNK, BB = A[:, 11008:12032], A[:, 12032:13056], A[:, 13056:14080]
        BON, LL, EE, RST = A[:, 14080:15104], A[:, 15104:16128], A[:, 16128:17152], A[:, 17152:18176]
        BT, KT, VT = TS, RNK, LL
        ABT, AKT, RBT, RKT = WW, AA, EE, RST
        TI, TIT = A[:, 18176:19200], A[:, 19200:20224]
        PX, MX = X[:, 2048:3072], X[:, 3072:4096]
        YY = BB
        RHS, SA, ST = SC[:, 0:256], SC[:, 256:512], SC[:, 512:1024]
        DC = SC[:, 1024:1040]
        HM = A[:, 2048:4096]
        CTB = A[0:NE, 4096:4352]
        CWB = A[:, 8192:16384]
        SGM = A[:, 4352:5376]
        LG = A[:, 5376:5504].rearrange("p (t e) -> p t e", t=2)

        ST3 = A[:, 15360:16896].rearrange("p (b t) -> p b t", b=3)
        SG = A[:, 6912:7936].rearrange("p (b t) -> p b t", b=2)
        TM = A[:, 7936:8448]
        MG = A[:, 8448:10496]
        RT = A[:, 5504:5888]
        CMB = A[:, 5888:5952].rearrange("p (t e) -> p t e", t=2)
        CT0 = A[:, 6144:6656]

        HSQ = SC[:, 0:1024].rearrange("p (b t) -> p b t", b=2)
        NM, SM = SC[:, 1280:1282], SC[:, 1282:1284]
        MX8 = SC[:, 1040:1056].rearrange("p (b t) -> p b t", b=2)
        SC3 = SC[:, 1284:1344]

        HN = [(Q1[:, c, :], vec("qk1", 0, 1), 256) for c in range(8)]
        HN += [(K1[:, c, :], vec("qk1", 1, 2), 512) for c in range(8)]
        HN += [(QA[:, c, :], vec("qk2", 0, 1), 256) for c in range(4)]
        HN += [(KA[:, c, :], vec("qk2", 1, 2), 256) for c in range(4)]

        ATT = [
            dict(n=2 * HEADS1, kc=4, q=Q1, k=K1, v=V1, p=P1B, pt=PT1, o=O1, tag="na", bias=None, u0=0),
            dict(n=2 * HEADS2, kc=2, q=QA, k=KA, v=VA, p=P2B, pt=PT2, o=OA, tag="dsa", bias=BI, u0=32),
        ]

        def bias_of(a, u):
            if a["bias"] is not None:
                return BI[:, u % 2, :]
            h, t = divmod(u, 2)
            o = (h * 6 + 2 * (1 - t)) * GRID_W
            return RPB[:, o:o + 256]

        WIN = {0: LATB[:, 0:256], 1: LATB[:, 256:512], 2: QI[:, 0, :], 3: QI[:, 1, :], 8: KI}
        for i in range(3):
            WIN[9 + i] = RP[:, i * 256:(i + 1) * 256]
        for i in range(12):
            WIN[12 + i] = RP[:, (3 + i) * 256:(4 + i) * 256]
        COPIES = sorted(WIN)

        def c64(ap, c, hp, h):
            o = (c * HP + hp) * 64
            return ap[64 * h:64 * h + 64, o:o + 64]

        def f64(ap, c, hp, h):
            o = hp * SEQ + c * CH
            return ap[64 * h:64 * h + 64, o:o + CH]

        def ps2(b, n=1024):
            return PS[:, b:b + n // 512, :].rearrange("p b t -> p (b t)")

        block = ctx.enter_context(nc.Block())

        @block.sync
        def _(sp):
            def load(stage, n):
                pl = plan[stage]
                s = n % pl["ring"]
                size = W[stage].shape[2]
                sp.dma_start(ring[:, s * pl["size"]:s * pl["size"] + size], W[stage][n]).then_inc(
                    sem(f"landed{s}"), 16)

            sig = {name: k for name, _, _, _, k in STREAM}

            def consumed(name, i):
                if name == "qkv":
                    if i < 4:
                        sp.wait_ge(sem("hn_mm"), 4 * (i + 1))
                    else:
                        sp.wait_ge(sem("v_mm"), 4 * (i - 3))
                elif name == "kvup":
                    sp.wait_ge(sem("va_mm"), 2)
                else:
                    sp.wait_ge(sem(f"mm_{name}"), sig[name] * (i + 1))

            for name, n, size, rg, k in STREAM:
                for i in range(min(n, rg)):
                    prev = plan[name]["first"][i]
                    if prev is not None:
                        consumed(*prev)
                    load(name, i)
                if name != "moe":
                    for i in range(rg, n):
                        consumed(name, i - rg)
                        load(name, i)
            with sp.Fori(1, NE // 2) as it:
                for s in range(6):
                    e, part = divmod(s, 3)
                    if part < 2:
                        sp.wait_ge(sem("gu_mm"), it * 8 + (4 * e + 2 * part - 6))
                    else:
                        sp.wait_ge(sem("dn_mm"), it * 2 + e)
                    sp.dma_start(ring[:, s * 4096:(s + 1) * 4096],
                                 W["moe"][bass.ds(it * 6 + s, 1), :, :].rearrange("a p n -> p (a n)")
                                 ).then_inc(sem(f"landed{s}"), 16)
            sp.wait_ge(sem("y_out"), 8)
            sp.dma_start(out, X[:, 0:2048]).then_inc(sem("stored"), 16)
            sp.wait_ge(sem("stored"), 16)

        @block.gpsimd
        def _(pool):
            pool.wait_ge(sem("mm_fout0"), 8)
            pool.dma_start(RPB, rpb).then_inc(sem("rpb_in"), 16)
            pool.dma_start(CM, colmask).then_inc(sem("cmask_in"), 16)
            pool.wait_ge(sem("rpb_in"), 16)
            pool.wait_ge(sem("cmask_in"), 16)
            pool.tensor_tensor(RPB.rearrange("p (r c) -> p r c", c=64), RPB.rearrange("p (r c) -> p r c", c=64),
                               CM.unsqueeze(1).to_broadcast([P, 96, 64]), ALU.add).then_inc(sem("bias_in"), 1)
            pool.wait_ge(sem("mm_fout1"), 8)
            pool.dma_start(DIST.rearrange("p c t -> p (c t)"), dist).then_inc(sem("dist_in"), 16)
            pool.wait_ge(sem("pv_dsa"), 16)
            pool.dma_start(RST, reset).then_inc(sem("reset_in"), 16)

        @block.scalar
        def _(act):
            cnt = [0]

            def link(ins):
                cnt[0] += 1
                ins.then_inc(sem("act_step"), 1)
                act.wait_ge(sem("act_step"), cnt[0])

            act.dma_start(V[:, :], vecs).then_inc(sem("vecs_in"), 16)
            act.dma_start(X[:, :], xin).then_inc(sem("x_in"), 16)
            act.dma_start(C[:, :], consts).then_inc(sem("consts_in"), 16)
            act.wait_ge(sem("vecs_in"), 16)
            act.activation(CS[:, :], vec("cs"), ACT.Silu).then_inc(sem("cond"), 1)
            act.wait_ge(sem("consts_in"), 16)
            act.wait_ge(sem("x_in"), 16)

            def norm(n):
                c0, layer, s2, cond = NORMS[n]
                T = s2 * SEQ
                act.activation(SQ[:, 0:8 * T], X[:, 0:8 * T], ACT.Square).then_inc(sem("sq_done"), 1)
                act.wait_ge(sem("stat_done"), n + 1)
                act.activation(RN[:, 0:T], PS[:, 7, 0:T], ACT.Sqrt, bias=eps, scale=1.0 / D).then_inc(
                    sem("root_done"), 1)
                for k in range(KD):
                    for s in range(s2):
                        act.wait_ge(sem("scaled"), HB[n] + k * s2 + s + 1)
                        h = H[:, k * T + s * SEQ:k * T + (s + 1) * SEQ]
                        act.activation(h, h, ACT.Identity, bias=mod(layer, c0 + k, cond + s)).then_inc(
                            sem("h_ready"), 1)

            def ffn_in(l):
                T = 2 * SEQ if l == 0 else SEQ
                with act.Fori(0, 2) as it:
                    for s in range(11):
                        act.wait_ge(sem(f"mm_fin{l}"), it * 11 + (s + 1))
                        b = s % 3
                        act.activation(ST3[:, b, 0:T], PS[:, 2 * b, 0:T], ACT.Silu).then_inc(sem("silu_done"), 1)

            def head_norm(i, bank):
                _, _, T = HN[i]
                if i < 16:
                    act.wait_ge(sem("hn_mm"), i + 1)
                elif i < 20:
                    act.wait_ge(sem("mm_win"), i - 16 + 5)
                else:
                    act.wait_ge(sem("hn_mm"), i - 4 + 1)
                if i >= 2:
                    act.wait_ge(sem("hn_done"), i - 1)
                act.activation(HSQ[:, i % 2, 0:T], PS[:, bank, 0:T], ACT.Square).then_inc(sem("hn_sq"), 1)

            def head_root(i, stat):
                _, _, T = HN[i]
                act.wait_ge(sem("hn_stat"), i + 1)
                is_q = i < 8 or 16 <= i < 20
                act.activation(HSQ[:, i % 2, 0:T], PS[:, stat, 0:T], ACT.Sqrt, bias=eps_q if is_q else eps,
                               scale=1.0 if is_q else 1.0 / HD).then_inc(sem("hn_root"), 1)

            def attention(a):
                t, n, u0 = a["tag"], a["n"], a["u0"]
                KT_ = a["kc"] * P

                def evict(u):
                    act.wait_ge(sem(f"tr_{t}"), u + 1)
                    if u >= 2:
                        act.wait_ge(sem(f"pv_{t}"), u - 1)
                    act.activation(a["pt"][:, u % 2, :], PS[:, 2 + u % 2, 0:KT_], ACT.Copy).then_inc(
                        sem(f"pt_{t}"), 1)

                for u in range(n):
                    act.wait_ge(sem(f"max_{t}"), u + 1)
                    if u >= 2:
                        act.wait_ge(sem(f"tr_{t}"), u - 1)
                    act.activation(a["p"][:, u % 2, :], PS[:, u % 2, 0:KT_], ACT.Exp, bias=NM[:, u % 2:u % 2 + 1],
                                   accum_out=SM[:, u % 2:u % 2 + 1]).then_inc(sem(f"exp_{t}"), 1)
                    if u >= 1:
                        evict(u - 1)
                evict(n - 1)

            norm(0)
            for j in range(KD):
                act.wait_ge(sem("mm_conv"), j + 1)
                if j >= 2:
                    act.wait_ge(sem("conv_done"), j - 1)
                act.activation(CT[:, (j % 2) * 512:(j % 2) * 512 + 512], PS[:, 3 * (j % 2) + 1, :], ACT.Copy).then_inc(
                    sem("c_copied"), 1)
            act.wait_ge(sem("res_done"), RB["fout0"])
            norm(1)
            ffn_in(0)
            act.wait_ge(sem("res_done"), RB["aout"])
            norm(2)
            for i in range(16):
                head_norm(i, i % 3)
                head_root(i, 3 + i % 2)
            for g in range(8):
                act.wait_ge(sem("v_mm"), g + 1)
                act.activation(V1[:, g % 4, (g // 4) * 512:(g // 4) * 512 + 512], PS[:, 5 + g % 3, :], ACT.Copy).then_inc(
                    sem("v_copied"), 1)
            attention(ATT[0])
            act.wait_ge(sem("res_done"), RB["fout1"])
            norm(3)
            ffn_in(1)
            act.wait_ge(sem("res_done"), RB["wout"])
            norm(4)
            for i in range(24):
                if 4 <= i < 8:
                    head_norm(16 + i - 4, i % 4)
                    head_root(16 + i - 4, 4 + i % 2)
                    continue
                act.wait_ge(sem("mm_win"), i + 1)
                act.activation(WIN[i], PS[:, i % 4, 0:SEQ], ACT.Copy).then_inc(sem("win_copied"), 1)
                if i == 1:
                    act.wait_ge(sem("win_copied"), 2)
                    act.activation(LSQ, LATB, ACT.Square).then_inc(sem("lat_sq"), 1)
                if i == 13:
                    act.wait_ge(sem("lat_stat"), 1)
                    act.activation(RN[:, 0:SEQ], PS[:, 6, 0:SEQ], ACT.Sqrt, bias=eps, scale=1.0 / LAT).then_inc(
                        sem("lat_root"), 1)
            act.wait_ge(sem("wi_mm"), 1)
            act.activation(SC3[:, 0:16], PS[:, 6, 256:272], ACT.Copy, scale=1.0 / 16.0).then_inc(sem("wi_done"), 1)
            for i in range(4):
                head_norm(20 + i, i)
                head_root(20 + i, 4 + i % 2)
            for t in range(2):
                act.wait_ge(sem("va_mm"), t + 1)
                act.activation(VA[:, t, :], PS[:, 6 + t, :], ACT.Copy).then_inc(sem("va_copied"), 1)
            for v in range(16):
                h = v % 8
                act.wait_ge(sem("dots"), v + 1)
                if v >= 4:
                    act.wait_ge(sem("scored"), v - 3)
                act.activation(RL[:, v % 4, :], PS[:, 4 + h % 4, 0:256], ACT.Relu).then_inc(
                    sem("relu"), 1)
            attention(ATT[1])

            act.wait_ge(sem("mixed"), 3)
            act.activation(RP[0:64, 0:256], RP[0:64, 0:256], ACT.Tanh).then_inc(sem("lora_in"), 1)
            act.activation(RP[:, 256:768], RP[:, 256:768], ACT.Sigmoid).then_inc(sem("lora_in"), 1)
            act.wait_ge(sem("lora_z"), 1)
            act.wait_ge(sem("mixed"), 15)
            for m in range(4):
                act.activation(WW[:, m * 256:(m + 1) * 256], PS[:, m // 2, (m % 2) * 256:(m % 2) * 256 + 256],
                               ACT.Sigmoid, bias=vec("w0", m, m + 1)).then_inc(sem("w_sig"), 1)
            act.wait_ge(sem("lora_a"), 1)
            for m in range(4):
                act.activation(AA[:, m * 256:(m + 1) * 256], PS[:, 2 + m // 2, (m % 2) * 256:(m % 2) * 256 + 256],
                               ACT.Sigmoid, bias=vec("a0", m, m + 1)).then_inc(sem("a_sig"), 1)
            act.wait_ge(sem("mm_lora"), 1)
            act.activation(GG, ps2(4), ACT.Copy).then_inc(sem("g_copied"), 1)
            act.wait_ge(sem("kk_raw"), 1)
            act.activation(TS, KK, ACT.Square).then_inc(sem("kk_sq"), 1)
            act.wait_ge(sem("kk_stat"), 1)
            act.activation(RNK, ps2(0), ACT.Sqrt).then_inc(sem("kk_root"), 1)
            act.wait_ge(sem("cum"), 1)
            act.activation(WW, WW, ACT.Exp).then_inc(sem("exp_prev"), 1)
            act.activation(EE, LL, ACT.Exp).then_inc(sem("exp_cum"), 1)
            act.wait_ge(sem("used_cum"), 1)
            act.activation(EE, LL, ACT.Exp, scale=-1.0).then_inc(sem("exp_inv"), 1)
            for i, dst in enumerate((BT, KT, VT)):
                act.wait_ge(sem("tok_mm"), i + 1)
                act.activation(dst, ps2((0, 2, 4)[i]), ACT.Copy).then_inc(sem("tok_copied"), 1)
            for lv in range(6):
                for b in range(2):
                    act.wait_ge(sem("p1_mm"), 2 * lv + b + 1)
                    act.activation(PX[:, b * 512:(b + 1) * 512], PS[:, b, :], ACT.Copy).then_inc(sem("p1_copied"), 1)
            for c in range(NCH):
                act.wait_ge(sem("rhs_mm"), c + 1)
                act.activation(RHS, PS[:, 0, 0:256], ACT.Copy).then_inc(sem("rhs_copied"), 1)
                act.wait_ge(sem("sa_mm"), c + 1)
                if c:
                    act.wait_ge(sem("y_mm"), c)
                act.activation(SA, PS[:, 1, 0:256], ACT.Copy, scale=-1.0).then_inc(sem("sa_copied"), 1)
            act.wait_ge(sem("y_mm"), NCH)
            act.activation(YY, ps2(6), ACT.Copy).then_inc(sem("y_copied"), 1)
            act.wait_ge(sem("centred"), 1)
            act.activation(TI, YY, ACT.Square).then_inc(sem("var_sq"), 1)
            act.wait_ge(sem("var_stat"), 1)
            act.activation(TIT, ps2(2), ACT.Sqrt, bias=gn_eps, scale=1.0 / HD).then_inc(sem("var_root"), 1)
            for m in range(KD):
                act.wait_ge(sem("mm_gates"), m + 1)
                if m >= 2:
                    act.wait_ge(sem("merged"), m - 1)
                act.activation(SG[:, m % 2, :], PS[:, 2 * (m % 2), :], ACT.Sigmoid).then_inc(sem("gate_sig"), 1)
            act.wait_ge(sem("res_done"), RB["end"])
            norm(5)
            act.wait_ge(sem("g_shift"), 1)
            act.activation(RT[:, 0:8], RT[:, 0:8], ACT.Exp).then_inc(sem("g_exp"), 1)
            act.wait_ge(sem("e_diff"), 1)
            act.activation(RT[:, 8:10], RT[:, 8:10], ACT.Exp).then_inc(sem("e_exp"), 1)
            for b in range(16):
                act.wait_ge(sem("cw_mm"), b + 1)
                act.activation(CWB[:, b * 512:(b + 1) * 512], PS[:, b % 4, :], ACT.Copy).then_inc(sem("cw_copied"), 1)
            with act.Fori(0, NE // 2) as it:
                for q in range(8):
                    act.wait_ge(sem("gu_mm"), it * 8 + (q + 1))
                    act.activation(SGM[:, (q % 4) * 256:(q % 4) * 256 + 256], PS[:, q % 4, 0:256], ACT.Silu).then_inc(
                        sem("m_silu"), 1)

        @block.tensor
        def _(pe):
            pe.wait_ge(sem("cond"), 1)
            pe.wait_ge(sem("consts_in"), 16)

            def ada(l):
                c = 1 if l == 2 else 0
                with pe.Fori(0, 2) as it:
                    for s in range(6):
                        slot_landed(pe, f"ada{l}", s, it)
                        if s == 0:
                            pe.wait_ge(sem("mod_read"), it + (2 * l + 1))
                        for m in range(4):
                            for k in range(KD):
                                mm = pe.matmul(PS[:, 7, (s * 4 + m) * 2:(s * 4 + m) * 2 + 2],
                                               slot("ada0", s, k * 512 + m * 128, k * 512 + m * 128 + 128),
                                               CS[:, 3 * k + c:3 * k + c + 2], start=(k == 0), stop=(k == KD - 1))
                        mm.then_inc(sem(f"mm_ada{l}"), 1)

            def norm(n):
                T = NORMS[n][2] * SEQ
                pe.wait_ge(sem("sq_done"), n + 1)
                if n in (0, 2, 4):
                    pe.wait_ge(sem("mod_read"), n + 3)
                for k in range(KD):
                    rhs = SQ[:, 0:8 * T].rearrange("p (s k t) -> p k s t", k=KD, t=SEQ)[:, k]
                    mm = pe.matmul(PS[:, 7, 0:T].rearrange("p (s t) -> p s t", t=SEQ), ones, rhs,
                                   start=(k == 0), stop=(k == KD - 1))
                mm.then_inc(sem("stat_done"), 1)

            def h_wait(n, k):
                pe.wait_ge(sem("h_ready"), HB[n] + (k + 1) * NORMS[n][2])

            def ffn(l):
                T = 2 * SEQ if l == 0 else SEQ
                stage = f"fin{l}"
                for k in range(KD):
                    h_wait(2 * l + 1, k)
                with pe.Fori(0, 2) as it:
                    for s in range(11):
                        slot_landed(pe, stage, s, it)
                        pe.wait_ge(sem("hid_done"), it * 11 + (s + (1 if s < 2 else 0)) + 22 * l)
                        for half in range(2):
                            for k in range(KD):
                                mm = pe.matmul(PS[:, 2 * (s % 3) + half, 0:T],
                                               slot(stage, s, k * 256 + half * 128, k * 256 + half * 128 + 128),
                                               h_of(k, T), start=(k == 0), stop=(k == KD - 1))
                        mm.then_inc(sem(f"mm_{stage}"), 1)
                pe.wait_ge(sem("hid_done"), 22 * (l + 1) + 2)
                stage = f"fout{l}"
                s2 = T // SEQ
                with pe.Fori(0, 2) as it:
                    for s in range(4):
                        slot_landed(pe, stage, s, it)
                        pe.wait_ge(sem("res_done"), it * 4 * s2 + (RB[stage] + (s - 3) * s2))
                        for k in range(KF):
                            mm = pe.matmul(PS[:, s, 0:T], slot(stage, s, k * 128, k * 128 + 128),
                                           HID[:, k * T:(k + 1) * T], start=(k == 0), stop=(k == KF - 1))
                        mm.then_inc(sem(f"mm_{stage}"), 1)

            def out_proj(stage, rhs_of, T):
                s2 = T // SEQ
                for m in range(KD):
                    if m % 4 == 0:
                        slot_landed(pe, stage, m // 4)
                    if m >= 4:
                        pe.wait_ge(sem("res_done"), RB[stage] + (m - 3) * s2)
                    for k in range(KD):
                        mm = pe.matmul(PS[:, m % 4, 0:T],
                                       slot(stage, m // 4, k * 512 + (m % 4) * 128, k * 512 + (m % 4) * 128 + 128),
                                       rhs_of(k), start=(k == 0), stop=(k == KD - 1))
                    mm.then_inc(sem(f"mm_{stage}"), 1)

            def head_stat(i, stat):
                T = HN[i][2]
                pe.wait_ge(sem("hn_sq"), i + 1)
                pe.matmul(PS[:, stat, 0:T], bo64, HSQ[:, i % 2, 0:T], start=True, stop=True).then_inc(sem("hn_stat"), 1)

            def attention(a):
                t, n, KC = a["tag"], a["n"], a["kc"]

                def scores(u):
                    h, tt = divmod(u, 2)
                    r = 64 * (h % 2)
                    if a["bias"] is not None:
                        pe.wait_ge(sem("bias_made"), u + 1)
                    if u >= 2:
                        pe.wait_ge(sem(f"exp_{t}"), u - 1)
                    pe.matmul(PS[:, u % 2, 0:KC * P], a["q"][r:r + 64, h // 2, tt * P:(tt + 1) * P],
                              a["k"][r:r + 64, h // 2, 0:KC * P], start=True, stop=False)
                    pe.matmul(PS[:, u % 2, 0:256], ident, bias_of(a, u), start=False, stop=True).then_inc(
                        sem(f"s_{t}"), 1)

                def turn(u):
                    pe.wait_ge(sem(f"p_{t}"), u + 1)
                    if u >= 2:
                        pe.wait_ge(sem(f"pt_{t}"), u - 1)
                    for kc in range(KC):
                        mm = pe.transpose(PS[:, 2 + u % 2, kc * P:(kc + 1) * P], a["p"][:, u % 2, kc * P:(kc + 1) * P],
                                          ident)
                    mm.then_inc(sem(f"tr_{t}"), 1)

                def pv(u):
                    h, tt = divmod(u, 2)
                    hp = h // 2
                    r = 64 * (h % 2)
                    pe.wait_ge(sem(f"pt_{t}"), u + 1)
                    if u % 4 == 0 and hp >= 2:
                        pe.wait_ge(sem(f"o_{t}"), hp - 1)
                    for kc in range(KC):
                        mm = pe.matmul(PS[r:r + 64, 4 + hp % 2, tt * P:(tt + 1) * P], a["v"][:, kc, h * 64:(h + 1) * 64],
                                       a["pt"][:, u % 2, kc * P:(kc + 1) * P], start=(kc == 0), stop=(kc == KC - 1))
                    mm.then_inc(sem(f"pv_{t}"), 1)

                scores(0)
                for u in range(n):
                    if u + 1 < n:
                        scores(u + 1)
                    turn(u)
                    if u >= 1:
                        pv(u - 1)
                pv(n - 1)

            ada(0)
            norm(0)
            for j in range(KD):
                slot_landed(pe, "conv", j)
                if j >= 2:
                    pe.wait_ge(sem("conv_done"), j - 1)
                for c in range(3):
                    for k in range(KD):
                        if j == 0 and c == 0:
                            h_wait(0, k)
                        mm = pe.matmul(PS[:, 3 * (j % 2) + c, :], slot("conv", j, k * 384 + c * 128, k * 384 + c * 128 + 128),
                                       h_of(k, 512), start=(k == 0), stop=(k == KD - 1))
                mm.then_inc(sem("mm_conv"), 1)
            pe.wait_ge(sem("conv_done"), KD)
            out_proj("cout", lambda k: YC[:, k * 512:(k + 1) * 512], 512)
            norm(1)
            ffn(0)
            ada(1)
            norm(2)
            for i in range(16):
                if i % 4 == 0:
                    slot_landed(pe, "qkv", i // 4)
                if i >= 3:
                    pe.wait_ge(sem("hn_done"), i - 2)
                T = HN[i][2]
                for k in range(KD):
                    if i == 0:
                        h_wait(2, k)
                    mm = pe.matmul(PS[:, i % 3, 0:T],
                                   slot("qkv", i // 4, k * 512 + (i % 4) * 128, k * 512 + (i % 4) * 128 + 128),
                                   h_of(k, 512)[:, 0:T], start=(k == 0), stop=(k == KD - 1))
                mm.then_inc(sem("hn_mm"), 1)
                if i >= 1:
                    head_stat(i - 1, 3 + (i - 1) % 2)
            for g in range(8):
                if g % 4 == 0:
                    slot_landed(pe, "qkv", 4 + g // 4)
                if g >= 3:
                    pe.wait_ge(sem("v_copied"), g - 2)
                for k in range(KD):
                    mm = pe.matmul(PS[:, 5 + g % 3, :], h_of(k, 512)[:, (g % 4) * P:(g % 4 + 1) * P],
                                   slot("qkv", 4 + g // 4, k * 512, k * 512 + 512), start=(k == 0), stop=(k == KD - 1))
                mm.then_inc(sem("v_mm"), 1)
                if g == 0:
                    head_stat(15, 3 + 1)
            pe.wait_ge(sem("v_copied"), 8)
            pe.wait_ge(sem("hn_done"), 16)
            pe.wait_ge(sem("bias_in"), 1)
            attention(ATT[0])
            pe.wait_ge(sem("o_na"), 8)
            out_proj("aout", lambda k: O1[:, k * SEQ:(k + 1) * SEQ], SEQ)
            norm(3)
            ffn(1)
            ada(2)
            norm(4)
            for i in range(24):
                if i % 4 == 0:
                    slot_landed(pe, "win", i // 4)
                if i >= 4:
                    if 8 <= i < 12:
                        pe.wait_ge(sem("hn_done"), 16 + i - 7)
                    else:
                        pe.wait_ge(sem("win_copied"), sum(c <= i - 4 for c in COPIES))
                for k in range(KD):
                    if i == 0:
                        h_wait(4, k)
                    mm = pe.matmul(PS[:, i % 4, 0:SEQ],
                                   slot("win", i // 4, k * 512 + (i % 4) * 128, k * 512 + (i % 4) * 128 + 128),
                                   XN[:, k * SEQ:(k + 1) * SEQ], start=(k == 0), stop=(k == KD - 1))
                mm.then_inc(sem("mm_win"), 1)
                if 5 <= i < 9:
                    head_stat(16 + i - 5, 4 + (i - 5) % 2)
                if i == 10:
                    pe.wait_ge(sem("lat_sq"), 1)
                    for c in range(2):
                        mm = pe.matmul(PS[:, 6, 0:SEQ], ones, LSQ[:, c * SEQ:(c + 1) * SEQ], start=(c == 0), stop=(c == 1))
                    mm.then_inc(sem("lat_stat"), 1)
                if i == 14:
                    pe.wait_ge(sem("lat_root"), 1)
                    for t in range(2):
                        for k in range(KD):
                            mm = pe.matmul(PS[:, 6, 256 + t * 8:264 + t * 8], XN[:, k * SEQ + t * P:k * SEQ + (t + 1) * P],
                                           vec("w_i", k * 8, k * 8 + 8), start=(k == 0), stop=(k == KD - 1))
                    mm.then_inc(sem("wi_mm"), 1)
            slot_landed(pe, "kvup", 0)
            pe.wait_ge(sem("lat_done"), 2)
            pe.wait_ge(sem("win_copied"), len(COPIES))
            pe.wait_ge(sem("hn_done"), 20)
            for i in range(4):
                for k in range(2):
                    mm = pe.matmul(PS[:, i, 0:SEQ], slot("kvup", 0, k * 1024 + i * 128, k * 1024 + i * 128 + 128),
                                   LATB[:, k * SEQ:(k + 1) * SEQ], start=(k == 0), stop=(k == 1))
                mm.then_inc(sem("hn_mm"), 1)
            for i in range(2):
                head_stat(20 + i, 4 + i)
            pe.wait_ge(sem("wi_done"), 1)
            for t in range(2):
                for k in range(2):
                    mm = pe.matmul(PS[:, 6 + t, :], LATB[:, k * SEQ + t * P:k * SEQ + (t + 1) * P],
                                   slot("kvup", 0, k * 1024 + 512, k * 1024 + 1024), start=(k == 0), stop=(k == 1))
                mm.then_inc(sem("va_mm"), 1)
            for i in range(2, 4):
                head_stat(20 + i, 4 + i % 2)
            pe.wait_ge(sem("va_copied"), 2)
            pe.wait_ge(sem("hn_done"), 24)
            for v in range(16):
                t, h = divmod(v, 8)
                r = 32 * (h % 4)
                if v >= 4:
                    pe.wait_ge(sem("relu"), v - 3)
                pe.matmul(PS[:, 4 + h % 4, 0:256], QI[r:r + 32, h // 4, t * P:(t + 1) * P],
                          KI[r:r + 32, :], start=True, stop=True, tile_position=(r, 0)).then_inc(sem("dots"), 1)
                if v == 15:
                    pe.wait_ge(sem("relu"), 16)
            attention(ATT[1])

            slot_landed(pe, "lora", 0)
            pe.wait_ge(sem("lora_in"), 2)
            pe.wait_ge(sem("o_dsa"), 4)
            for m in range(4):
                mm = pe.matmul(PS[:, m // 2, (m % 2) * 256:(m % 2) * 256 + 256], slot("lora", 0, m * 128, m * 128 + 128, 0, 64),
                               RP[0:64, 0:256], start=True, stop=True)
            mm.then_inc(sem("lora_z"), 1)
            for m in range(4):
                mm = pe.matmul(PS[:, 2 + m // 2, (m % 2) * 256:(m % 2) * 256 + 256],
                               slot("lora", 0, m * 128, m * 128 + 128, 64, 128), RP[64:128, 0:256], start=True, stop=True)
            mm.then_inc(sem("lora_a"), 1)
            for m in range(4):
                dst = PS[:, 4 + m // 2, (m % 2) * 256:(m % 2) * 256 + 256]
                pe.matmul(dst, slot("lora", 0, 512 + m * 128, 640 + m * 128), RP[:, 256:512], start=True, stop=False)
                mm = pe.matmul(dst, slot("lora", 0, 1024 + m * 128, 1152 + m * 128), RP[:, 512:768], start=False, stop=True)
            mm.then_inc(sem("mm_lora"), 1)
            pe.wait_ge(sem("kk_sq"), 1)
            for b in range(2):
                mm = pe.matmul(PS[:, b, :], bo64, TS[:, b * 512:(b + 1) * 512], start=True, stop=True)
            mm.then_inc(sem("kk_stat"), 1)
            pe.wait_ge(sem("rk_made"), 1)
            for b in range(2):
                mm = pe.matmul(PS[:, 2 + b, :], bo64, EE[:, b * 512:(b + 1) * 512], start=True, stop=True)
            mm.then_inc(sem("rk_sum"), 1)
            for i, (src, ready) in enumerate(((BB, "b_hat"), (RK, "k_hat"), (RV, "k_hat"))):
                pe.wait_ge(sem(ready), 1)
                for c in range(NCH):
                    for hp in range(HP):
                        for h in range(2):
                            b = 2 * i + c // 2
                            o = ((c % 2) * HP + hp) * 64
                            mm = pe.matmul(PS[64 * h:64 * h + 64, b, o:o + 64], f64(src, c, hp, h),
                                           con("id64")[64 * h:64 * h + 64, :], start=True, stop=True)
                mm.then_inc(sem("tok_mm"), 1)
            for i, (left, right) in enumerate(((BB, KK), (RK, KK), (BB, RR), (RK, RR))):
                b0 = (6, 0, 2, 4)[i]
                if i:
                    pe.wait_ge(sem("tok_copied"), i)
                for c in range(NCH):
                    for hp in range(HP):
                        for h in range(2):
                            b = b0 + c // 2
                            o = ((c % 2) * HP + hp) * 64
                            mm = pe.matmul(PS[64 * h:64 * h + 64, b, o:o + 64], f64(left, c, hp, h),
                                           f64(right, c, hp, h), start=True, stop=True)
                mm.then_inc(sem("tri_mm"), 1)
            for lv in range(6):
                if lv == 0:
                    pe.wait_ge(sem("tri_masked"), 8)
                for b in range(2):
                    pe.wait_ge(sem("lv_masked"), lv + 1)
                    for c in range(2 * b, 2 * b + 2):
                        for hp in range(HP):
                            for h in range(2):
                                o = ((c % 2) * HP + hp) * 64
                                mm = pe.matmul(PS[64 * h:64 * h + 64, b, o:o + 64], c64(MX, c, hp, h),
                                               c64(TI, c, hp, h), start=True, stop=True)
                    mm.then_inc(sem("p1_mm"), 1)
                for b in range(2):
                    pe.wait_ge(sem("p1_copied"), 2 * lv + b + 1)
                    for c in range(2 * b, 2 * b + 2):
                        for hp in range(HP):
                            for h in range(2):
                                o = ((c % 2) * HP + hp) * 64
                                pe.matmul(PS[64 * h:64 * h + 64, 2 + b, o:o + 64], c64(TIT, c, hp, h),
                                          c64(PX, c, hp, h), start=True, stop=True)
                                mm = pe.matmul(PS[64 * h:64 * h + 64, 4 + b, o:o + 64], c64(PX, c, hp, h),
                                               c64(TIT, c, hp, h), start=True, stop=True)
                    mm.then_inc(sem("p2_mm"), 1)
            pe.wait_ge(sem("t_done"), 24)
            for c in range(NCH):
                st = ST[:, (c % 2) * 256:(c % 2) * 256 + 256]
                if c:
                    pe.wait_ge(sem("state"), c)
                for hp in range(HP):
                    for h in range(2):
                        dst = PS[64 * h:64 * h + 64, 0, hp * 64:hp * 64 + 64]
                        if c:
                            pe.matmul(dst, f64(KK, c, hp, h), st[64 * h:64 * h + 64, hp * 64:hp * 64 + 64],
                                      start=True, stop=False)
                        mm = pe.matmul(dst, c64(AKT, c, hp, h), c64(VT, c, hp, h), start=(c == 0), stop=True)
                mm.then_inc(sem("rhs_mm"), 1)
                pe.wait_ge(sem("rhs_copied"), c + 1)
                for hp in range(HP):
                    for h in range(2):
                        mm = pe.matmul(PS[64 * h:64 * h + 64, 1, hp * 64:hp * 64 + 64], c64(TIT, c, hp, h),
                                       RHS[64 * h:64 * h + 64, hp * 64:hp * 64 + 64], start=True, stop=True)
                mm.then_inc(sem("sa_mm"), 1)
                pe.wait_ge(sem("sa_copied"), c + 1)
                for hp in range(HP):
                    for h in range(2):
                        dst = PS[64 * h:64 * h + 64, 2, hp * 64:hp * 64 + 64]
                        pe.matmul(dst, c64(BT, c, hp, h), SA[64 * h:64 * h + 64, hp * 64:hp * 64 + 64],
                                  start=True, stop=False)
                        mm = pe.matmul(dst, c64(KT, c, hp, h), c64(VT, c, hp, h), start=False, stop=True)
                mm.then_inc(sem("state_mm"), 1)
                for hp in range(HP):
                    for h in range(2):
                        o = (hp % 2) * 256 + c * CH
                        dst = PS[64 * h:64 * h + 64, 6 + hp // 2, o:o + CH]
                        if c:
                            pe.matmul(dst, st[64 * h:64 * h + 64, hp * 64:hp * 64 + 64], f64(RR, c, hp, h),
                                      start=True, stop=False)
                        pe.matmul(dst, SA[64 * h:64 * h + 64, hp * 64:hp * 64 + 64], c64(RBT, c, hp, h),
                                  start=(c == 0), stop=False)
                        mm = pe.matmul(dst, c64(VT, c, hp, h), c64(RKT, c, hp, h), start=False, stop=True)
                mm.then_inc(sem("y_mm"), 1)
            pe.wait_ge(sem("y_copied"), 1)
            for b in range(2):
                mm = pe.matmul(PS[:, b, :], bo64, YY[:, b * 512:(b + 1) * 512], start=True, stop=True)
            mm.then_inc(sem("mean_sum"), 1)
            pe.wait_ge(sem("var_sq"), 1)
            pe.wait_ge(sem("state"), NCH)
            for b in range(2):
                mm = pe.matmul(PS[:, 2 + b, :], bo64, TI[:, b * 512:(b + 1) * 512], start=True, stop=True)
            mm.then_inc(sem("var_stat"), 1)
            pe.wait_ge(sem("o_rwkv"), 1)
            for m in range(KD):
                slot_landed(pe, "gates", m)
                if m >= 2:
                    pe.wait_ge(sem("merged"), m - 1)
                b = 2 * (m % 2)
                for g in range(2):
                    for k in range(KD):
                        pe.matmul(PS[:, b, g * 256:g * 256 + 256], slot("gates", m, g * 1024 + k * 128, g * 1024 + k * 128 + 128),
                                  XN[:, k * SEQ:(k + 1) * SEQ], start=(k == 0), stop=(k == KD - 1))
                for g, o in enumerate((OA, YY)):
                    for k in range(4):
                        w = 2048 + g * 512 + k * 128
                        mm = pe.matmul(PS[:, b + 1, g * 256:g * 256 + 256], slot("gates", m, w, w + 128),
                                       o[:, k * SEQ:(k + 1) * SEQ], start=(k == 0), stop=(k == 3))
                mm.then_inc(sem("mm_gates"), 1)
            pe.wait_ge(sem("merged"), KD)
            out_proj("wout", lambda k: MG[:, k * SEQ:(k + 1) * SEQ], SEQ)
            norm(5)
            for k in range(KD):
                h_wait(5, k)
            pe.wait_ge(sem("root_done"), 6)
            for t in range(2):
                for k in range(KD):
                    mm = pe.matmul(PS[:, 6, t * 64:t * 64 + 36], XN[:, k * SEQ + t * P:k * SEQ + (t + 1) * P],
                                   vec("router", k * 36, k * 36 + 36), start=(k == 0), stop=(k == KD - 1))
            mm.then_inc(sem("logits"), 1)
            pe.wait_ge(sem("combined"), 1)
            for t in range(2):
                mm = pe.transpose(PS[0:NE, 5, t * P:(t + 1) * P], CMB[:, t, :], ident)
            mm.then_inc(sem("cmb_mm"), 1)
            pe.wait_ge(sem("cmb_copied"), 1)
            for e in range(NE):
                if e % 2 == 0 and e >= 8:
                    pe.wait_ge(sem("cw_copied"), e // 2 - 3)
                mm = pe.matmul(PS[:, (e // 2) % 4, (e % 2) * 256:(e % 2) * 256 + 256],
                               ident[0:NE, e:e + 1].to_broadcast([NE, P]), CTB, start=True, stop=True)
                if e % 2:
                    mm.then_inc(sem("cw_mm"), 1)
            pe.wait_ge(sem("cw_copied"), 16)
            pe.wait_ge(sem("zeros"), 1)
            for b in range(4):
                pe.matmul(PS[:, 4 + b, :], ident, CT0, start=True, stop=True)
            with pe.Fori(0, NE // 2) as it:
                def gate_up(e, q):
                    s = 3 * e + q // 2
                    if q % 2 == 0:
                        slot_landed(pe, "moe", s, it)
                    pe.wait_ge(sem("hm_done"), it * 8 + (4 * e + q + 1))
                    for g in range(2):
                        for k in range(KD):
                            w = k * 512 + (2 * (q % 2) + g) * 128
                            mm = pe.matmul(PS[:, q, g * 256:g * 256 + 256], slot("moe", s, w, w + 128),
                                           XN[:, k * SEQ:(k + 1) * SEQ], start=(k == 0), stop=(k == KD - 1))
                    mm.then_inc(sem("gu_mm"), 1)

                def down(e):
                    slot_landed(pe, "moe", 3 * e + 2, it)
                    for m in range(KD):
                        for q in range(4):
                            if m == 0:
                                pe.wait_ge(sem("hm_done"), it * 8 + (4 * e + q + 5))
                            mm = pe.matmul(PS[:, 4 + m // 2, (m % 2) * 256:(m % 2) * 256 + 256],
                                           slot("moe", 3 * e + 2, q * 1024 + m * 128, q * 1024 + m * 128 + 128),
                                           HM[:, e * 1024 + q * 256:e * 1024 + q * 256 + 256],
                                           start=False, stop=False, skip_group_check=True)
                    return mm

                for e in range(2):
                    for q in range(4):
                        gate_up(e, q)
                    down(e).then_inc(sem("dn_mm"), 1)

        @block.vector
        def _(dve):
            cnt = [0]

            def link(ins):
                cnt[0] += 1
                ins.then_inc(sem("dve_step"), 1)
                dve.wait_ge(sem("dve_step"), cnt[0])

            dve.wait_ge(sem("vecs_in"), 16)
            dve.wait_ge(sem("consts_in"), 16)
            dve.wait_ge(sem("x_in"), 16)
            dve.memset(SC3[:, 0:1], 0.0).then_inc(sem("hid_done"), 2)
            dve.memset(SC3[:, 1:2], 0.0).then_inc(sem("hm_done"), 4)
            dve.memset(SC3[:, 2:3], 0.0).then_inc(sem("mod_read"), 1)
            dve.memset(SC3[:, 3:4], 0.0).then_inc(sem("dn_mm"), 1)

            def ada(l):
                for it in range(2):
                    dve.wait_ge(sem(f"mm_ada{l}"), 6 * (it + 1))
                    o = l * 96 + it * 48
                    dve.tensor_tensor(MOD[:, o:o + 48].rearrange("p (m c) -> p m c", c=2),
                                      PS[:, 7, 0:48].rearrange("p (m c) -> p m c", c=2),
                                      vec("b_ada", l * 48 + it * 24, l * 48 + it * 24 + 24).unsqueeze(2).to_broadcast([P, 24, 2]),
                                      ALU.add).then_inc(sem("mod_read"), 1)
                dve.wait_ge(sem("mod_read"), 2 * l + 3)
                for i in range(2):
                    n = 2 * l + i
                    link(dve.scalar_tensor_tensor(
                        out=AB[:, n * 16:n * 16 + 16].rearrange("p (k c) -> p k c", c=2), in0=mod2(l, 8 + 24 * i), scalar=1.0,
                        in1=vec("g_norm", n * 8, n * 8 + 8).unsqueeze(2).to_broadcast([P, 8, 2]), op0=ALU.add, op1=ALU.mult))

            def norm(n):
                _, _, s2, cond = NORMS[n]
                T = s2 * SEQ
                dve.wait_ge(sem("root_done"), n + 1)
                link(dve.reciprocal(RN[:, 0:T], RN[:, 0:T]))
                for k in range(KD):
                    for s in range(s2):
                        a = n * 16 + 2 * k + cond + s
                        dve.scalar_tensor_tensor(out=H[:, k * T + s * SEQ:k * T + (s + 1) * SEQ],
                                                 in0=X[:, s * 2048 + k * SEQ:s * 2048 + (k + 1) * SEQ], scalar=AB[:, a:a + 1],
                                                 in1=RN[:, s * SEQ:(s + 1) * SEQ], op0=ALU.mult, op1=ALU.mult).then_inc(
                            sem("scaled"), 1)

            def residual(i):
                stage, c0, layer, s2 = RES[i]
                for m in range(KD):
                    dve.wait_ge(sem(f"mm_{stage}"), m + 1)
                    for s in range(s2):
                        xs = X[:, s * 2048 + m * SEQ:s * 2048 + (m + 1) * SEQ]
                        dve.scalar_tensor_tensor(out=xs, in0=PS[:, m % 4, s * SEQ:(s + 1) * SEQ],
                                                 scalar=mod(layer, c0 + m, (1 if layer == 2 else 0) + s), in1=xs,
                                                 op0=ALU.mult, op1=ALU.add).then_inc(sem("res_done"), 1)

            def ffn_in(l):
                T = 2 * SEQ if l == 0 else SEQ
                with dve.Fori(0, 2) as it:
                    for s in range(11):
                        dve.wait_ge(sem("silu_done"), it * 11 + (22 * l + s + 1))
                        b = s % 3
                        dve.tensor_tensor(HID[:, bass.ds((it * 11 + s) * T, T)], ST3[:, b, 0:T], PS[:, 2 * b + 1, 0:T],
                                          ALU.mult).then_inc(sem("hid_done"), 1)

            def head_norm(i, bank):
                dst, gain, T = HN[i]
                dve.wait_ge(sem("hn_root"), i + 1)
                link(dve.reciprocal(HSQ[:, i % 2, 0:T], HSQ[:, i % 2, 0:T]))
                dve.scalar_tensor_tensor(out=dst, in0=PS[:, bank, 0:T], scalar=gain, in1=HSQ[:, i % 2, 0:T],
                                         op0=ALU.mult, op1=ALU.mult).then_inc(sem("hn_done"), 1)

            def attention(a):
                t, n, KC = a["tag"], a["n"], a["kc"]

                def bias(u):
                    h, tt = divmod(u, 2)
                    if u >= 2:
                        dve.wait_ge(sem(f"s_{t}"), u - 1)
                    dve.scalar_tensor_tensor(out=BI[:, u % 2, :], in0=DIST[:, tt, :], scalar=-(2.0 ** -(h + 1)),
                                             in1=SEL[:, tt, :], op0=ALU.mult, op1=ALU.add).then_inc(sem("bias_made"), 1)

                def row_max(u):
                    dve.wait_ge(sem(f"s_{t}"), u + 1)
                    dve.tensor_reduce(NM[:, u % 2:u % 2 + 1], PS[:, u % 2, 0:KC * P], AX.X, ALU.max, negate=True).then_inc(
                        sem(f"max_{t}"), 1)

                def scale(u):
                    dve.wait_ge(sem(f"exp_{t}"), u + 1)
                    link(dve.reciprocal(SM[:, u % 2:u % 2 + 1], SM[:, u % 2:u % 2 + 1]))
                    pb = a["p"][:, u % 2, :]
                    dve.tensor_scalar(pb, pb, SM[:, u % 2:u % 2 + 1], None, ALU.mult).then_inc(sem(f"p_{t}"), 1)

                def out_copy(hp):
                    dve.wait_ge(sem(f"pv_{t}"), 4 * hp + 4)
                    dve.tensor_copy(a["o"][:, hp * SEQ:(hp + 1) * SEQ], PS[:, 4 + hp % 2, 0:SEQ]).then_inc(sem(f"o_{t}"), 1)

                if a["bias"] is not None:
                    bias(0)
                    bias(1)
                row_max(0)
                for u in range(n):
                    if a["bias"] is not None and u + 2 < n:
                        bias(u + 2)
                    scale(u)
                    if u + 1 < n:
                        row_max(u + 1)
                    if u >= 5 and (u - 5) % 4 == 0:
                        out_copy((u - 5) // 4)
                out_copy(n // 4 - 1)

            ada(0)
            norm(0)
            link(dve.memset(A[:, 9216:9732], 0.0))
            for j in range(KD):
                dve.wait_ge(sem("c_copied"), j + 1)
                if j:
                    dve.wait_ge(sem("conv_done"), j)
                b = 3 * (j % 2)
                w = [vec("conv_w", i * 8 + j, i * 8 + j + 1) for i in range(3)]
                ct = CT[:, (j % 2) * 512:(j % 2) * 512 + 512].rearrange("p (s t) -> p s t", s=2)
                link(dve.tensor_tensor(Z[:, :, 1:257], ct, PS[:, b + 2, :].rearrange("p (s t) -> p s t", s=2), ALU.mult))
                link(dve.tensor_scalar(T1, Z[:, :, 0:256], w[0], None, ALU.mult))
                link(dve.scalar_tensor_tensor(out=T1, in0=Z[:, :, 1:257], scalar=w[1], in1=T1, op0=ALU.mult, op1=ALU.add))
                link(dve.scalar_tensor_tensor(out=T1, in0=Z[:, :, 2:258], scalar=w[2], in1=T1, op0=ALU.mult, op1=ALU.add))
                dve.tensor_tensor(YC[:, j * 512:(j + 1) * 512].rearrange("p (s t) -> p s t", s=2),
                                  PS[:, b, :].rearrange("p (s t) -> p s t", s=2), T1, ALU.mult).then_inc(sem("conv_done"), 1)
            residual(0)
            norm(1)
            ffn_in(0)
            residual(1)
            ada(1)
            norm(2)
            for i in range(16):
                head_norm(i, i % 3)
            attention(ATT[0])
            residual(2)
            norm(3)
            ffn_in(1)
            residual(3)
            ada(2)
            norm(4)
            for i in range(4):
                head_norm(16 + i, i)
            dve.wait_ge(sem("lat_root"), 1)
            link(dve.reciprocal(RN[:, 0:SEQ], RN[:, 0:SEQ]))
            for c in range(2):
                la = LATB[:, c * SEQ:(c + 1) * SEQ]
                dve.scalar_tensor_tensor(out=la, in0=la, scalar=vec("g_lat", c, c + 1), in1=RN[:, 0:SEQ], op0=ALU.mult,
                                         op1=ALU.mult).then_inc(sem("lat_done"), 1)
            for i in range(4):
                head_norm(20 + i, i)
            dve.wait_ge(sem("dist_in"), 16)
            dve.wait_ge(sem("wi_done"), 1)
            link(dve.tensor_scalar(NEGM, DIST, 0.0, NEG, ALU.is_lt, ALU.mult))
            for v in range(16):
                t, h = divmod(v, 8)
                dve.wait_ge(sem("relu"), v + 1)
                prev = NEGM if h == 0 else SCO
                if v:
                    dve.wait_ge(sem("scored"), v)
                dve.scalar_tensor_tensor(out=SCO[:, t, :], in0=RL[:, v % 4, :], scalar=SC3[:, v:v + 1], in1=prev[:, t, :],
                                         op0=ALU.mult, op1=ALU.add).then_inc(sem("scored"), 1)
            dve.wait_ge(sem("scored"), 16)
            for r in range(TOPK // 8):
                dve.max(MX8[:, 0, :], SCO[:, 0, :]).then_inc(sem("top"), 1)
                dve.max(MX8[:, 1, :], SCO[:, 1, :]).then_inc(sem("top"), 1)
                dve.wait_ge(sem("top"), 2 * r + 2)
                link(dve.match_replace(SCO[:, 0, :], MX8[:, 0, :], SCO[:, 0, :], -3e38))
                link(dve.match_replace(SCO[:, 1, :], MX8[:, 1, :], SCO[:, 1, :], -3e38))
            link(dve.tensor_scalar(SEL, SCO, -2e38, NEG, ALU.is_gt, ALU.mult))
            link(dve.tensor_tensor(SEL, SEL, NEGM, ALU.add))
            attention(ATT[1])

            p3 = RP.rearrange("p (c t) -> p c t", t=SEQ)
            d3 = DF.rearrange("p (c t) -> p c t", t=SEQ)
            dve.wait_ge(sem("pv_dsa"), 16)
            dve.wait_ge(sem("win_copied"), len(COPIES))
            link(dve.tensor_tensor(d3[:, :, 1:SEQ], p3[:, :, 0:SEQ - 1], p3[:, :, 1:SEQ], ALU.subtract))
            link(dve.tensor_scalar(d3[:, :, 0:1], p3[:, :, 0:1], -1.0, None, ALU.mult))
            for c in range(15):
                ins = dve.scalar_tensor_tensor(out=p3[:, c, :], in0=d3[:, c, :], scalar=vec("mu", c, c + 1), in1=p3[:, c, :],
                                               op0=ALU.mult, op1=ALU.add)
                ins.then_inc(sem("mixed"), 1)
            dve.wait_ge(sem("mixed"), 15)

            for m in range(4):
                sl = slice(m * 256, (m + 1) * 256)
                link(dve.tensor_scalar(KK[:, sl], RK[:, sl], vec("k_k", m, m + 1), None, ALU.mult))
            dve.memset(SC3[:, 32:33], 0.0).then_inc(sem("kk_raw"), 1)
            dve.wait_ge(sem("w_sig"), 4)
            link(dve.tensor_scalar(WW, WW, -float(np.exp(-0.5)), None, ALU.mult))
            dve.wait_ge(sem("reset_in"), 16)
            link(dve.tensor_tensor_scan(LL, RST, WW, 0.0, ALU.mult, ALU.add))
            dve.tensor_tensor(WW, LL, WW, ALU.subtract).then_inc(sem("w_prev"), 1)
            dve.wait_ge(sem("a_sig"), 4)
            dve.wait_ge(sem("kk_root"), 1)
            for m in range(4):
                sl = slice(m * 256, (m + 1) * 256)
                link(dve.tensor_scalar(TS[:, sl], AA[:, sl], -1.0, vec("k_a", m, m + 1), ALU.add, ALU.mult))
                link(dve.scalar_tensor_tensor(out=RK[:, sl], in0=TS[:, sl], scalar=1.0, in1=RK[:, sl], op0=ALU.add,
                                              op1=ALU.mult))
            for m in range(4):
                sl = slice(m * 256, (m + 1) * 256)
                ins = dve.scalar_tensor_tensor(out=EE[:, sl], in0=RR[:, sl], scalar=vec("r_k", m, m + 1), in1=RK[:, sl],
                                               op0=ALU.mult, op1=ALU.mult)
                link(ins)
            dve.memset(SC3[:, 33:34], 0.0).then_inc(sem("rk_made"), 1)
            link(dve.tensor_scalar(RNK, RNK, 1e-12, None, ALU.max))
            link(dve.reciprocal(RNK, RNK))
            link(dve.tensor_tensor(KK, KK, RNK, ALU.mult))
            link(dve.tensor_tensor(BB, KK, AA, ALU.mult))
            dve.wait_ge(sem("rk_sum"), 1)
            dve.wait_ge(sem("w_prev"), 1)
            link(dve.tensor_tensor(BON, ps2(2), RV, ALU.mult))
            dve.memset(SC3[:, 34:35], 0.0).then_inc(sem("cum"), 1)
            dve.wait_ge(sem("exp_prev"), 1)
            link(dve.tensor_tensor(KK, KK, WW, ALU.mult))
            dve.wait_ge(sem("exp_cum"), 1)
            link(dve.tensor_tensor(RR, RR, EE, ALU.mult))
            dve.tensor_copy(DC.rearrange("p (c h) -> p h c", h=HP),
                            EE.rearrange("p (h c t) -> p h c t", h=HP, c=NCH)[:, :, :, CH - 1]).then_inc(sem("used_cum"), 1)
            dve.wait_ge(sem("exp_inv"), 1)
            dve.tensor_tensor(BB, BB, EE, ALU.mult).then_inc(sem("b_hat"), 1)
            dve.tensor_tensor(RK, RK, EE, ALU.mult).then_inc(sem("k_hat"), 1)
            for i, (dst, mask) in enumerate(((ABT, "strict"), (AKT, "strict"), (RBT, "incl"), (RKT, "incl"))):
                b0 = (6, 0, 2, 4)[i]
                dve.wait_ge(sem("tri_mm"), i + 1)
                if i == 0:
                    dve.wait_ge(sem("k_hat"), 1)
                    dve.wait_ge(sem("b_hat"), 1)
                for b in range(2):
                    dve.tensor_tensor(dst[:, b * 512:(b + 1) * 512].rearrange("p (c t) -> p c t", t=64),
                                      PS[:, b0 + b, :].rearrange("p (c t) -> p c t", t=64),
                                      con(mask).unsqueeze(1).to_broadcast([P, 8, 64]), ALU.mult).then_inc(sem("tri_masked"), 1)
            dve.wait_ge(sem("tri_masked"), 8)
            idb = con("id64").unsqueeze(1).to_broadcast([P, 16, 64])
            link(dve.tensor_copy(TI.rearrange("p (c t) -> p c t", t=64), idb))
            link(dve.tensor_copy(TIT.rearrange("p (c t) -> p c t", t=64), idb))
            for lv in range(6):
                if lv:
                    dve.wait_ge(sem("t_done"), 4 * lv)
                dve.tensor_tensor(MX.rearrange("p (c t) -> p c t", t=64), ABT.rearrange("p (c t) -> p c t", t=64),
                                  con("level", lv * 64, lv * 64 + 64).unsqueeze(1).to_broadcast([P, 16, 64]),
                                  ALU.mult).then_inc(sem("lv_masked"), 1)
                for b in range(2):
                    sl = slice(b * 512, (b + 1) * 512)
                    dve.wait_ge(sem("p2_mm"), 2 * lv + b + 1)
                    dve.tensor_tensor(TI[:, sl], TI[:, sl], PS[:, 2 + b, :], ALU.subtract).then_inc(sem("t_done"), 1)
                    dve.tensor_tensor(TIT[:, sl], TIT[:, sl], PS[:, 4 + b, :], ALU.subtract).then_inc(sem("t_done"), 1)
            for c in range(NCH):
                old = ST[:, (c % 2) * 256:(c % 2) * 256 + 256]
                new = ST[:, (1 - c % 2) * 256:(1 - c % 2) * 256 + 256]
                dcb = DC[:, c * HP:(c + 1) * HP].unsqueeze(2).to_broadcast([P, HP, 64])
                n3 = new.rearrange("p (h j) -> p h j", h=HP)
                dve.wait_ge(sem("state_mm"), c + 1)
                if c:
                    dve.wait_ge(sem("y_mm"), c)
                    link(dve.tensor_tensor(new, PS[:, 2, 0:256], old, ALU.add))
                    dve.tensor_tensor(n3, n3, dcb, ALU.mult).then_inc(sem("state"), 1)
                else:
                    dve.tensor_tensor(n3, PS[:, 2, 0:256].rearrange("p (h j) -> p h j", h=HP), dcb, ALU.mult).then_inc(
                        sem("state"), 1)
                dve.wait_ge(sem("state"), c + 1)
            dve.wait_ge(sem("mean_sum"), 1)
            dve.scalar_tensor_tensor(out=YY, in0=ps2(0), scalar=-1.0 / HD, in1=YY, op0=ALU.mult, op1=ALU.add).then_inc(
                sem("centred"), 1)
            dve.wait_ge(sem("var_root"), 1)
            dve.wait_ge(sem("centred"), 1)
            link(dve.reciprocal(TIT, TIT))
            link(dve.tensor_tensor(YY, YY, TIT, ALU.mult))
            for m in range(4):
                sl = slice(m * 256, (m + 1) * 256)
                link(dve.tensor_scalar(YY[:, sl], YY[:, sl], vec("ln_w", m, m + 1), vec("ln_b", m, m + 1), ALU.mult, ALU.add))
            link(dve.tensor_tensor(YY, YY, BON, ALU.add))
            dve.wait_ge(sem("g_copied"), 1)
            dve.tensor_tensor(YY, YY, GG, ALU.mult).then_inc(sem("o_rwkv"), 1)
            for m in range(KD):
                dve.wait_ge(sem("gate_sig"), m + 1)
                if m:
                    dve.wait_ge(sem("merged"), m)
                link(dve.tensor_tensor(TM, SG[:, m % 2, :], PS[:, 2 * (m % 2) + 1, :], ALU.mult))
                dve.tensor_tensor(MG[:, m * SEQ:(m + 1) * SEQ], TM[:, 0:256], TM[:, 256:512], ALU.add).then_inc(
                    sem("merged"), 1)
            residual(4)
            norm(5)
            dve.wait_ge(sem("logits"), 1)
            link(dve.tensor_copy(LG[:, :, 0:36], PS[:, 6, 0:128].rearrange("p (t e) -> p t e", t=2)[:, :, 0:36]))
            G, E = LG[:, :, 0:4], LG[:, :, 4:36]
            link(dve.tensor_tensor(E, E, vec("e_bias").unsqueeze(1).to_broadcast([P, 2, NE]), ALU.add))
            small = RT[:, 8:32]
            gexp = RT[:, 0:8].rearrange("p (t e) -> p t e", t=2)
            oh = [RT[:, 64 + 64 * i:128 + 64 * i].rearrange("p (t e) -> p t e", t=2) for i in range(4)]

            def two(i):
                return small[:, 2 * i:2 * i + 2]

            def wide(i, w):
                return two(i).unsqueeze(2).to_broadcast([P, 2, w])

            def first_max(v, w, m, dst):
                link(dve.tensor_reduce(two(m), v, AX.X, ALU.max))
                link(dve.tensor_tensor(dst, v, wide(m, w), ALU.is_equal))
                link(dve.tensor_scalar(dst, dst, -99.0, 99.0, ALU.mult, ALU.add))
                link(dve.tensor_tensor(dst, dst, con("iota", 0, w).unsqueeze(1).to_broadcast([P, 2, w]), ALU.add))
                link(dve.tensor_reduce(two(11), dst, AX.X, ALU.min))
                link(dve.tensor_tensor(dst, dst, wide(11, w), ALU.is_equal))

            goh = oh[0][:, :, 0:4]
            first_max(G, 4, 1, goh)
            dve.tensor_tensor(gexp, G, wide(1, 4), ALU.subtract).then_inc(sem("g_shift"), 1)
            link(dve.tensor_scalar(goh, goh, -NEG, NEG, ALU.mult, ALU.add))
            link(dve.tensor_tensor(E.rearrange("p t (g e) -> p t g e", g=4), E.rearrange("p t (g e) -> p t g e", g=4),
                                   goh.unsqueeze(3).to_broadcast([P, 2, 4, EPG]), ALU.add))
            first_max(E, NE, 2, oh[1])
            link(dve.scalar_tensor_tensor(out=E, in0=oh[1], scalar=-3e38, in1=E, op0=ALU.mult, op1=ALU.add))
            first_max(E, NE, 3, oh[2])
            dve.tensor_tensor(two(0), two(3), two(2), ALU.subtract).then_inc(sem("e_diff"), 1)
            dve.wait_ge(sem("g_exp"), 1)
            link(dve.tensor_reduce(two(4), gexp, AX.X, ALU.add))
            dve.wait_ge(sem("e_exp"), 1)
            link(dve.scalar_tensor_tensor(out=two(5), in0=two(0), scalar=1.0, in1=two(4), op0=ALU.add, op1=ALU.mult))
            link(dve.reciprocal(two(6), two(5)))
            link(dve.tensor_tensor(two(7), two(6), two(0), ALU.mult))
            link(dve.tensor_tensor(oh[1], oh[1], wide(6, NE), ALU.mult))
            link(dve.tensor_tensor(oh[2], oh[2], wide(7, NE), ALU.mult))
            dve.tensor_tensor(CMB, oh[1], oh[2], ALU.add).then_inc(sem("combined"), 1)
            dve.memset(CT0, 0.0).then_inc(sem("zeros"), 1)
            dve.wait_ge(sem("cmb_mm"), 1)
            dve.tensor_copy(CTB, PS[0:NE, 5, 0:SEQ]).then_inc(sem("cmb_copied"), 1)
            dve.wait_ge(sem("cw_copied"), 16)
            with dve.Fori(0, NE // 2) as it:
                for e in range(2):
                    for q in range(4):
                        dve.wait_ge(sem("m_silu"), it * 8 + (4 * e + q + 1))
                        if q == 0:
                            dve.wait_ge(sem("dn_mm"), it * 2 + 1)
                        sg = SGM[:, q * 256:q * 256 + 256]
                        dve.tensor_tensor(sg, sg, CWB[:, bass.ds((it * 2 + e) * 256, 256)], ALU.mult).then_inc(
                            sem("m_cw"), 1)
                        dve.wait_ge(sem("m_cw"), it * 8 + (4 * e + q + 1))
                        dve.tensor_tensor(HM[:, e * 1024 + q * 256:e * 1024 + q * 256 + 256], sg, PS[:, q, 256:512],
                                          ALU.mult).then_inc(sem("hm_done"), 1)
            dve.wait_ge(sem("dn_mm"), NE + 1)
            for m in range(KD):
                xs = X[:, m * SEQ:(m + 1) * SEQ]
                dve.scalar_tensor_tensor(out=xs, in0=PS[:, 4 + m // 2, (m % 2) * 256:(m % 2) * 256 + 256],
                                         scalar=mod(2, 40 + m, 1), in1=xs, op0=ALU.mult, op1=ALU.add).then_inc(
                    sem("y_out"), 1)


def feature_major(a):
    t, f = a.shape
    return a.T.reshape(f // P, P, t).transpose(1, 0, 2).reshape(P, -1)


def columns(v):
    return v.reshape(-1, P).T


def tiles(w, per_slot):
    k, m = w.shape
    return w.reshape(k // P, P, m // (per_slot * P), per_slot * P).transpose(2, 1, 0, 3).reshape(
        m // (per_slot * P), P, -1)


def chunks_in_order(w, order):
    k, m = w.shape
    return w.reshape(k, m // P, P)[:, order].reshape(k, -1)


def host_consts():
    c = np.zeros((P, NCONST), np.float32)
    i = np.arange(P)
    r, t = i[:, None] % 64, np.arange(64)[None, :]

    def put(name, a):
        c[:, COFF[name]:COFF[name] + a.shape[1]] = a

    put("ident", np.eye(P))
    put("ones", np.ones((P, P)))
    put("bo64", (i[:, None] // 64 == i[None, :] // 64) * 1.0)
    put("id64", (r == t) * 1.0)
    put("strict", (r < t) * 1.0)
    put("incl", (r <= t) * 1.0)
    lv = []
    for n in range(6):
        b = 1 << n
        lv.append((r // (2 * b) == t // (2 * b)) & (r % (2 * b) < b) & (t % (2 * b) >= b))
    put("level", np.concatenate(lv, 1) * 1.0)
    put("iota", np.broadcast_to(np.arange(32.0), (P, 32)))
    put("eps", np.broadcast_to(np.array([EPS, GN_EPS, EPS * HD]), (P, 3)))
    q = np.arange(P)[:, None] % GRID_W
    k = np.arange(GRID_W)[None, :]
    start = np.clip(q - NA_COLS // 2, 0, GRID_W - NA_COLS)
    colmask = np.where((k >= start) & (k < start + NA_COLS), 0.0, NEG).astype(np.float32)
    tok = np.arange(SEQ)
    dist = np.concatenate([np.arange(P)[:, None] + P * t2 - tok[None, :] for t2 in range(2)], 1).astype(np.float32)
    reset = np.broadcast_to((np.arange(HP * SEQ) % CH != 0).astype(np.float32), (P, HP * SEQ)).copy()
    return c, colmask, dist, reset


def kernel(**inp):
    import concourse.bacc as bacc
    from concourse.bass_utils import run_bass_kernel_spmd

    a = {k: np.asarray(v) for k, v in inp.items()}
    cat = np.concatenate

    shift_w = 1824
    r_w = 512
    mu = a["rwkv_mu_2"][0]

    def shift_cols(w, axis):
        r_, k_, v_, wl, al, gl = np.split(w, [512, 1024, 1536, 1600, 1664], axis=axis)
        pad = np.zeros(w.shape[:axis] + (96,) + w.shape[axis + 1:], w.dtype)
        return cat([wl, al, gl, pad, r_, k_, v_], axis=axis)

    two = lambda g: np.concatenate([g, g])[:, None]
    router = cat([a["router_group_w_2"][0], a["router_expert_w_2"][0]], 1)
    w_in = a["w_in_2"][0]
    q_a, kv, q_i, k_i, w_i, shf, g_a, g_r = np.split(w_in, np.cumsum([512, 256, 256, 32, 8, shift_w, 1024]), axis=1)
    cs = np.stack([columns(a["c"][0]), columns(a["c_ctx"]), columns(a["c_2"][0])], 2).reshape(P, 24)
    parts = {
        "b_ada": cat([columns(a["b_ada"][0]), columns(a["b_ada"][1]), columns(a["ada_b_2"][0])], 1),
        "g_norm": cat([columns(v) for v in (a["norm_mix"][0], a["norm_ffn"][0], a["norm_mix"][1], a["norm_ffn"][1],
                                            a["mix_norm_g_2"][0], a["moe_norm_g_2"][0])], 1),
        "conv_w": cat([columns(a["conv_w"][0, i]) for i in range(3)], 1),
        "qk1": cat([two(a["attn_q_norm"][0]), two(a["attn_k_norm"][0])], 1),
        "qk2": cat([two(a["q_norm_g_2"][0]), two(a["k_norm_g_2"][0])], 1),
        "g_lat": columns(a["kv_norm_g_2"][0]),
        "mu": columns(shift_cols(mu, 0)),
        "w0": columns(a["rwkv_w0_2"][0]), "a0": columns(a["rwkv_a0_2"][0]), "k_k": columns(a["rwkv_k_k_2"][0]),
        "k_a": columns(a["rwkv_k_a_2"][0]), "r_k": columns(a["rwkv_r_k_2"][0].reshape(-1)),
        "ln_w": columns(a["rwkv_ln_w_2"][0]), "ln_b": columns(a["rwkv_ln_b_2"][0]),
        "cs": cs,
        "e_bias": np.broadcast_to(a["router_expert_bias_2"][0][None], (P, NE)),
        "w_i": tiles_small(w_i), "router": tiles_small(router),
    }
    vecs = cat([parts[n] for n, _ in VECS], 1)

    conv_order = [x for j in range(8) for x in (j, 8 + j, 16 + j)]
    gu_order = [x for j in range(KF) for x in (j, KF + j)]
    wi = cat([kv, q_i, q_a, k_i, k_i, k_i, k_i, shift_cols(shf, 1)], 1)
    qkv = a["attn_w_qkv"][0]
    lora = cat([cat([a["rwkv_w2_2"][0], a["rwkv_a2_2"][0]], 0), a["rwkv_g2_2"][0][:128],
                cat([a["rwkv_g2_2"][0][128:], np.zeros((96, 512), np.float32)], 0)], 1)[None]
    ga, gr, ba, br = (tiles(w, 1) for w in (g_a, g_r, a["w_branch_attn_2"][0], a["w_branch_rwkv_2"][0]))
    wg, wu, wd = a["expert_w_gate_2"][0], a["expert_w_up_2"][0], a["expert_w_down_2"][0]
    gu = np.stack([wg.reshape(NE, KD, P, 4, P), wu.reshape(NE, KD, P, 4, P)], 4)
    gu = gu.reshape(NE, KD, P, 2, 2, 2, P).transpose(0, 3, 2, 1, 4, 5, 6).reshape(NE, 2, P, 4096)
    dn = wd.reshape(NE, 4, P, D).transpose(0, 2, 1, 3).reshape(NE, 1, P, 4096)
    W = {
        "ada0": tiles(a["w_ada"][0], 4), "ada1": tiles(a["w_ada"][1], 4), "ada2": tiles(a["ada_w_2"][0], 4),
        "conv": tiles(chunks_in_order(a["conv_w_in"][0], conv_order), 3), "cout": tiles(a["conv_w_out"][0], 4),
        "fin0": tiles(chunks_in_order(a["ffn_w_in"][0], gu_order), 2), "fout0": tiles(a["ffn_w_out"][0], 1),
        "fin1": tiles(chunks_in_order(a["ffn_w_in"][1], gu_order), 2), "fout1": tiles(a["ffn_w_out"][1], 1),
        "qkv": tiles(qkv, 4), "aout": tiles(a["attn_w_out"][0], 4),
        "win": tiles(wi, 4), "kvup": tiles(a["w_kv_up_2"][0], 8), "lora": lora,
        "gates": cat([ga, gr, ba, br], 2), "wout": tiles(a["w_out_2"][0], 4),
        "moe": cat([gu, dn], 1).reshape(NE * 3, P, 4096),
    }
    rp = np.stack([a["attn_rpb"][0][:, 5:11, :], a["attn_rpb"][0][:, 4:10, :]])
    pad = (GRID_W - 1) - (NA_COLS - 1)
    rp = np.pad(rp, ((0, 0), (0, 0), (0, 0), (pad, pad)))
    c, colmask, dist, reset = host_consts()
    xin = cat([feature_major(a["x"][0]), feature_major(a["ctx"][0])], 1)

    nc = bacc.Bacc("TRN2", target_bir_lowering=False, num_devices=1)
    arrays, aps = {}, {}

    def give(name, arr):
        arr = np.ascontiguousarray(arr)
        arrays[name] = arr
        aps[name] = nc.dram_tensor(name, arr.shape, F32, kind="ExternalInput").ap()
        return aps[name]

    Wap = {k: give(f"w_{k}", v) for k, v in W.items()}
    out = nc.dram_tensor("out", (P, 2048), F32, kind="ExternalOutput").ap()
    slide = np.arange(GRID_W)[None, :] - np.arange(GRID_W)[:, None] + GRID_W - 1
    table = rp[:, :, :, slide].transpose(0, 3, 1, 2, 4).reshape(P, -1)
    build(nc, give("xin", xin), give("vecs", vecs), give("consts", c), give("colmask", colmask), give("dist", dist),
          give("reset", reset), give("rpb", table), Wap, out)
    r = run_bass_kernel_spmd(nc, [arrays], core_ids=[0])
    y = r.results[0]["out"]
    return y.reshape(P, KD, SEQ).transpose(2, 1, 0).reshape(1, SEQ, D)


def tiles_small(w):
    return w.reshape(KD, P, -1).transpose(1, 0, 2).reshape(P, -1)
```

```python
from contextlib import ExitStack

import numpy as np

import concourse.bass as bass
from concourse import mybir

F32 = mybir.dt.float32
ALU = mybir.AluOpType
ACT = mybir.ActivationFunctionType
AX = mybir.AxisListType

P = 128
D = 1024
KD = D // P
SEQ = 256
FH = 2816
KF = FH // P
EPS = 1e-6
GN_EPS = 64e-5
NEG = -1e30
GRID_W, NA_ROWS, NA_COLS = 64, 8, 16
HEADS1 = 16
HEADS2 = 8
HD = 64
LAT = 256
TOPK = 64
NE = 32
EPG = 8
CAP = 64
CH = 64
NCH = SEQ // CH
HP = HEADS2 // 2
RING = 24576
GRP = 512
NG = 6 * D // GRP
PE_G = 1
PARTS = 4
PG_BASE = [0, NG - PE_G, 2 * NG - PE_G, 3 * NG - PE_G]

STREAM = [
    ("ada0", 1, 4096, 6, 1),
    ("conv", 8, 3072, 7, 1),
    ("cout", 2, 4096, 6, 4),
    ("fin0", 22, 2048, 11, 1),
    ("fout0", 8, 2816, 4, 1),
    ("qkv", 6, 4096, 6, 4),
    ("aout", 2, 4096, 6, 4),
    ("fin1", 22, 2048, 11, 1),
    ("fout1", 8, 2816, 4, 1),
    ("win", 6, 4096, 6, 4),
    ("kvup", 1, 2048, 1, 1),
    ("lora", 1, 1536, 1, 1),
    ("gates", 8, 3072, 8, 1),
    ("wout", 2, 4096, 6, 4),
    ("moe", 96, 4096, 6, 1),
]


def count_products():
    before, total = {}, 0
    for name, n, _, _, signals in STREAM:
        if name not in ("qkv", "kvup", "moe"):
            before[name] = total
            total += n * signals
    return before


def plan_stream():
    plan, owners, count, shared = {}, [], [0] * 11, {}
    for name, n, size, ring, _ in STREAM:
        first = []
        for s in range(min(n, ring)):
            a, b = s * size, (s + 1) * size
            hit = [o for o in owners if o[0] < b and a < o[1]] + [shared[k] for k in (s,) if k in shared]
            first.append(max(hit, key=lambda o: o[2])[3:] if hit else None)
        plan[name] = dict(n=n, size=size, ring=ring, first=first, base=list(count))
        for s in range(min(n, ring)):
            last = max(i for i in range(n) if i % ring == s)
            a, b = s * size, (s + 1) * size
            owners = [o for o in owners if not (a <= o[0] and o[1] <= b)]
            owners.append((a, b, len(plan) * 1000 + last, name, last))
            shared[s] = owners[-1]
            count[s] += 16 * (last // ring + 1)
    return plan


VECS = [
    ("b_ada", 144), ("g_norm", 48), ("conv_w", 24), ("qk1", 2), ("qk2", 2), ("g_lat", 2),
    ("mu", 15), ("w0", 4), ("a0", 4), ("k_k", 4), ("k_a", 4), ("r_k", 4), ("ln_w", 4), ("ln_b", 4),
    ("cs", 24), ("e_bias", 32), ("w_i", 64), ("router", 288),
]
VOFF, _o = {}, 0
for _n, _w in VECS:
    VOFF[_n] = _o
    _o += _w
NVEC = _o
CONSTS = [("ident", 128), ("ones", 128), ("bo64", 128), ("id64", 64), ("strict", 64), ("incl", 64),
          ("level", 384), ("iota", 32), ("eps", 3)]
COFF, _o = {}, 0
for _n, _w in CONSTS:
    COFF[_n] = _o
    _o += _w
NCONST = _o


def build(nc, xin, ada, vecs, consts, colmask, dist, reset, rpb, rank_c, W, out):
    plan = plan_stream()
    MMB = count_products()
    with ExitStack() as ctx:
        def sb(name, cols):
            return ctx.enter_context(nc.sbuf_tensor(name, [P, cols], F32))

        sems = {}

        def sem(name):
            if name not in sems:
                sems[name] = ctx.enter_context(nc.semaphore(name))
            return sems[name]

        ring = sb("ring", RING)
        X = sb("X", 4096)
        A = sb("A", 20480)
        C = sb("C", NCONST)
        V = sb("V", NVEC)
        MOD = sb("MOD", 3 * 96)
        AB = sb("AB", 6 * 16)
        CS = sb("CS", 24)
        RN = sb("RN", 512)
        CM = sb("CM", 64)[:, :]
        SC = sb("SC", 1344)
        PS = ctx.enter_context(nc.psum_tensor("PS", [P, 8, 512], F32))

        def con(name, a=0, b=None):
            w = dict(CONSTS)[name]
            return C[:, COFF[name] + a:COFF[name] + (w if b is None else b)]

        def vec(name, a=0, b=None):
            w = dict(VECS)[name]
            return V[:, VOFF[name] + a:VOFF[name] + (w if b is None else b)]

        ident, ones, bo64 = con("ident"), con("ones"), con("bo64")
        eps, gn_eps, eps_q = (con("eps", i, i + 1) for i in range(3))

        def slot(stage, s, a, b, p0=0, p1=P):
            o = plan[stage]["size"] * (s % plan[stage]["ring"])
            return ring[p0:p1, o + a:o + b]

        def slot_landed(eng, stage, s, turn=0):
            r = s % plan[stage]["ring"]
            eng.wait_ge(sem(f"landed{r}"), plan[stage]["base"][r] + 16 * (turn + s // plan[stage]["ring"] + 1))

        def mod(layer, chunk, cond):
            o = layer * 96 + chunk * 2 + cond
            return MOD[:, o:o + 1]

        def mod2(layer, c0):
            return MOD[:, layer * 96 + 2 * c0:layer * 96 + 2 * (c0 + 8)].rearrange("p (k c) -> p k c", c=2)

        NORMS = [(0, 0, 2, 0), (24, 0, 2, 0), (0, 1, 2, 0), (24, 1, 1, 0), (0, 2, 1, 1), (24, 2, 1, 1)]
        HB = [0]
        for nn in NORMS:
            HB.append(HB[-1] + 8 * nn[2])
        H = A[:, 0:4096]

        RES = [("cout", 16, 0, 2), ("fout0", 40, 0, 2), ("aout", 16, 1, 1), ("fout1", 40, 1, 1),
               ("wout", 16, 2, 1)]
        RB, _r = {}, 0
        for stage, _, _, s2 in RES:
            RB[stage] = _r
            _r += 8 * s2
        RB["end"] = _r

        def h_of(k, T):
            return H[:, k * T:(k + 1) * T]

        ADA = [ring[:, RING - 2048:RING - 1024], ring[:, RING - 1024:RING], A[:, 16896:17920], A[:, 17920:18944]]
        ACC = SC[:, 0:2 * GRP].rearrange("p (c w) -> p c w", c=2)

        HID = A[:, 4096:15360]
        SQ = H

        YC = A[:, 4096:8192]
        CT = A[:, 8192:9216]
        Z = A[:, 9216:9732].rearrange("p (s t) -> p s t", s=2)
        T1 = A[:, 9732:10244].rearrange("p (s t) -> p s t", s=2)
        Q1 = A[:, 4096:6144].rearrange("p (c t) -> p c t", c=8)
        K1 = A[:, 6144:10240].rearrange("p (c t) -> p c t", c=8)
        V1 = A[:, 10240:14336].rearrange("p (c t) -> p c t", c=4)
        RPB = A[:, 14336:20480]
        P1B = A[:, 0:1024].rearrange("p (b t) -> p b t", b=2)
        PT1 = A[:, 1024:2048].rearrange("p (b t) -> p b t", b=2)
        O1 = A[:, 2048:4096]
        XN = A[:, 0:2048]
        RP = A[:, 2048:5888]
        OA = A[:, 5888:6912]
        LATB = A[:, 6912:7424]
        QA = A[:, 7424:8448].rearrange("p (c t) -> p c t", c=4)
        KA = A[:, 8448:9472].rearrange("p (c t) -> p c t", c=4)
        VA = A[:, 9472:10496].rearrange("p (c t) -> p c t", c=2)
        QI = A[:, 10496:11008].rearrange("p (c t) -> p c t", c=2)
        KI = A[:, 11008:11264]
        SCO = A[:, 11264:11776].rearrange("p (c t) -> p c t", c=2)
        NEGM = A[:, 11776:12288].rearrange("p (c t) -> p c t", c=2)
        SEL = A[:, 12288:12800].rearrange("p (c t) -> p c t", c=2)
        DIST = A[:, 12800:13312].rearrange("p (c t) -> p c t", c=2)
        BI = A[:, 13312:13824].rearrange("p (b t) -> p b t", b=2)
        P2B = A[:, 13824:14336].rearrange("p (b t) -> p b t", b=2)
        PT2 = A[:, 14336:14848].rearrange("p (b t) -> p b t", b=2)
        RL = A[:, 14848:15872].rearrange("p (b t) -> p b t", b=4)
        LSQ = A[:, 15872:16384]
        RR, RK, RV = A[:, 2816:3840], A[:, 3840:4864], A[:, 4864:5888]
        DF = A[:, 16384:20224]
        WW, AA, GG, KK = A[:, 6912:7936], A[:, 7936:8960], A[:, 8960:9984], A[:, 9984:11008]
        TS, RNK, BB = A[:, 11008:12032], A[:, 12032:13056], A[:, 13056:14080]
        BON, LL, EE, RST = A[:, 14080:15104], A[:, 15104:16128], A[:, 16128:17152], A[:, 17152:18176]
        BT, KT, VT = TS, RNK, LL
        ABT, AKT, RBT, RKT = WW, AA, EE, RST
        TI, TIT = A[:, 18176:19200], A[:, 19200:20224]
        PX, MX = X[:, 2048:3072], X[:, 3072:4096]
        YY = BB
        RHS, SA, ST = SC[:, 0:256], SC[:, 256:512], SC[:, 512:1024]
        DC = SC[:, 1024:1040]
        HM = A[:, 2048:4096]
        CTB = A[0:NE, 4096:4352]
        CWB = A[:, 8192:16384]
        SGM = A[:, 4352:5376]
        XT = A[:, 2048:4096].rearrange("p (t d) -> p t d", t=2)
        PG = A[:, 8192:12544].rearrange("p (t s) -> p t s", t=2)
        PTS = A[:, 12544:16896]
        PCW = A[:, 16896:18944]
        XG, HF, YS = A[:, 16896:17920], A[:, 17920:18432], A[:, 18432:19456]
        SGF = A[:, 19456:19968]
        UPPER, IOTA64 = X[:, 2048:2176], X[:, 2176:2240]
        RANK = SC[:, 0:64].rearrange("p (t e) -> p t e", t=2)
        IND = SC[:, 64:128].rearrange("p (t e) -> p t e", t=2)
        FLAG = ctx.enter_context(nc.sbuf_tensor("FLAG", [P, 1], mybir.dt.int32))
        LG = A[:, 5376:5504].rearrange("p (t e) -> p t e", t=2)

        ST3 = A[:, 15360:16896].rearrange("p (b t) -> p b t", b=3)
        SG = A[:, 6912:7936].rearrange("p (b t) -> p b t", b=2)
        TM = A[:, 7936:8448]
        MG = A[:, 8448:10496]
        RT = A[:, 5504:5888]
        CMB = A[:, 5888:5952].rearrange("p (t e) -> p t e", t=2)
        CT0 = A[:, 6144:6656]

        HSQ = SC[:, 0:1024].rearrange("p (b t) -> p b t", b=2)
        NM, SM = SC[:, 1280:1282], SC[:, 1282:1284]
        MX8 = SC[:, 1040:1056].rearrange("p (b t) -> p b t", b=2)
        SC3 = SC[:, 1284:1344]

        HN = [(Q1[:, c, :], vec("qk1", 0, 1), 256) for c in range(8)]
        HN += [(K1[:, c, :], vec("qk1", 1, 2), 512) for c in range(8)]
        HN += [(QA[:, c, :], vec("qk2", 0, 1), 256) for c in range(4)]
        HN += [(KA[:, c, :], vec("qk2", 1, 2), 256) for c in range(4)]

        ATT = [
            dict(n=2 * HEADS1, kc=4, q=Q1, k=K1, v=V1, p=P1B, pt=PT1, o=O1, tag="na", bias=None, u0=0),
            dict(n=2 * HEADS2, kc=2, q=QA, k=KA, v=VA, p=P2B, pt=PT2, o=OA, tag="dsa", bias=BI, u0=32),
        ]

        def bias_of(a, u):
            if a["bias"] is not None:
                return BI[:, u % 2, :]
            h, t = divmod(u, 2)
            o = (h * 6 + 2 * (1 - t)) * GRID_W
            return RPB[:, o:o + 256]

        WIN = {0: LATB[:, 0:256], 1: LATB[:, 256:512], 2: QI[:, 0, :], 3: QI[:, 1, :], 8: KI}
        for i in range(3):
            WIN[9 + i] = RP[:, i * 256:(i + 1) * 256]
        for i in range(12):
            WIN[12 + i] = RP[:, (3 + i) * 256:(4 + i) * 256]
        COPIES = sorted(WIN)

        def c64(ap, c, hp, h):
            o = (c * HP + hp) * 64
            return ap[64 * h:64 * h + 64, o:o + 64]

        def f64(ap, c, hp, h):
            o = hp * SEQ + c * CH
            return ap[64 * h:64 * h + 64, o:o + CH]

        def ps2(b, n=1024):
            return PS[:, b:b + n // 512, :].rearrange("p b t -> p (b t)")

        def count_of(eng):
            eng.wait_ge(sem("counted"), 1)
            return eng.value_load(FLAG[0:1, 0:1], min_val=0, max_val=SEQ)

        block = ctx.enter_context(nc.Block())

        @block.sync
        def _(sp):
            def load(stage, n):
                pl = plan[stage]
                s = n % pl["ring"]
                size = W[stage].shape[2]
                sp.dma_start(ring[:, s * pl["size"]:s * pl["size"] + size], W[stage][n]).then_inc(
                    sem(f"landed{s}"), 16)

            sp.wait_ge(sem("vecs_in"), 16)
            sp.wait_ge(sem("consts_in"), 16)
            sig = {name: k for name, _, _, _, k in STREAM}

            def consumed(name, i):
                if name == "qkv":
                    if i < 4:
                        sp.wait_ge(sem("hn_mm"), 4 * (i + 1))
                    else:
                        sp.wait_ge(sem("v_mm"), 4 * (i - 3))
                elif name == "kvup":
                    sp.wait_ge(sem("va_mm"), 2)
                else:
                    sp.wait_ge(sem("product"), MMB[name] + (sig[name] * (i + 1)))

            for name, n, size, rg, k in STREAM:
                if name == "conv":
                    sp.wait_ge(sem("ada_in3"), 16 * (4 - PE_G))
                for i in range(min(n, rg)):
                    prev = plan[name]["first"][i]
                    if prev is not None:
                        consumed(*prev)
                    if name in ("qkv", "win") and i == 5:
                        groups = PG_BASE[2 if name == "qkv" else 3]
                        sp.wait_ge(sem("ada_step"), 2 * KD * min(groups, PG_BASE[2]) + KD * (groups - min(groups, PG_BASE[2])))
                    load(name, i)
                if name != "moe":
                    for i in range(rg, n):
                        consumed(name, i - rg)
                        load(name, i)
            with sp.Fori(1, NE // 2) as it:
                for s in range(6):
                    if s < 4:
                        sp.wait_ge(sem("gu_mm"), it * 8 + (2 * s - 6))
                    else:
                        sp.wait_ge(sem("dn_mm"), it * 2 + (s - 4))
                    sp.dma_start(ring[:, s * 4096:(s + 1) * 4096],
                                 W["moe"][bass.ds(it * 6 + s, 1), :, :].rearrange("a p n -> p (a n)")
                                 ).then_inc(sem(f"landed{s}"), 16)
            sp.wait_ge(sem("y_out"), 8)
            sp.dma_start(out, X[:, 0:2048]).then_inc(sem("stored"), 16)
            sp.wait_ge(sem("stored"), 16)

        @block.gpsimd
        def _(pool):
            def group_loads(it, n):
                for q in range(PARTS):
                    src = ada[n * PARTS + q]
                    if it is not None:
                        two = n < PG_BASE[2]
                        before = 2 * KD * min(n, PG_BASE[2]) + KD * max(n - PG_BASE[2], 0)
                        step = 2 * KD if two else KD
                        pool.wait_ge(sem("ada_step"), it * step + (before - step + (q + 1) * (step // PARTS)))
                        src = ada[bass.ds(it * PARTS + (n * PARTS + q), 1), :, :].rearrange("a p w -> p (a w)")
                    pool.dma_start(ADA[q], src).then_inc(sem(f"ada_in{q}"), 16)

            group_loads(None, 0)
            with pool.Fori(0, PG_BASE[2] - 1) as it:
                group_loads(it, 1)
            pool.wait_ge(sem("product"), MMB["fout0"] + (8))
            pool.dma_start(RPB, rpb).then_inc(sem("rpb_in"), 16)
            pool.dma_start(CM, colmask).then_inc(sem("cmask_in"), 16)
            pool.wait_ge(sem("rpb_in"), 16)
            pool.wait_ge(sem("cmask_in"), 16)
            pool.tensor_tensor(RPB.rearrange("p (r c) -> p r c", c=64), RPB.rearrange("p (r c) -> p r c", c=64),
                               CM.unsqueeze(1).to_broadcast([P, 96, 64]), ALU.add).then_inc(sem("bias_in"), 1)
            pool.wait_ge(sem("s_na"), 2 * HEADS1)
            pool.wait_ge(sem("ada_step"), 2 * KD * PG_BASE[2])
            pool.wait_ge(sem("v_mm"), 8)
            group_loads(None, PG_BASE[2])
            with pool.Fori(0, NG - 1) as it:
                group_loads(it, PG_BASE[2] + 1)
            pool.wait_ge(sem("product"), MMB["fout1"] + (8))
            pool.dma_start(DIST.rearrange("p c t -> p (c t)"), dist).then_inc(sem("dist_in"), 16)
            p3 = RP.rearrange("p (c t) -> p c t", t=SEQ)
            d3 = DF.rearrange("p (c t) -> p c t", t=SEQ)
            mu = vec("mu").unsqueeze(2).to_broadcast([P, 15, SEQ])
            pool.wait_ge(sem("win_copied"), len(COPIES))
            pool.wait_ge(sem("lat_done"), 2)
            pool.tensor_tensor(d3[:, :, 1:SEQ], p3[:, :, 0:SEQ - 1], p3[:, :, 1:SEQ], ALU.subtract).then_inc(sem("mixed"), 1)
            pool.tensor_scalar(d3[:, :, 0:1], p3[:, :, 0:1], -1.0, None, ALU.mult).then_inc(sem("mixed"), 1)
            pool.wait_ge(sem("mixed"), 2)
            pool.tensor_tensor(d3, d3, mu, ALU.mult).then_inc(sem("mixed"), 1)
            pool.wait_ge(sem("mixed"), 3)
            pool.tensor_tensor(RP, RP, DF, ALU.add).then_inc(sem("mixed"), 2)
            pool.wait_ge(sem("mixed"), 5)
            pool.wait_ge(sem("pv_dsa"), 16)
            pool.dma_start(RST, reset).then_inc(sem("reset_in"), 16)
            pool.wait_ge(sem("o_rwkv"), 1)
            pool.dma_start(X[:, 2048:2240], rank_c).then_inc(sem("rank_in"), 16)

        @block.scalar
        def _(act):
            cnt = [0]

            def link(ins):
                cnt[0] += 1
                ins.then_inc(sem("act_step"), 1)
                act.wait_ge(sem("act_step"), cnt[0])

            act.dma_start(V[:, :], vecs).then_inc(sem("vecs_in"), 16)
            act.dma_start(C[:, :], consts).then_inc(sem("consts_in"), 16)
            act.wait_ge(sem("vecs_in"), 16)
            act.activation(CS[:, :], vec("cs"), ACT.Silu).then_inc(sem("cond"), 1)
            slot_landed(act, "ada0", 0)
            act.dma_start(X[:, :], xin).then_inc(sem("x_in"), 16)
            act.wait_ge(sem("consts_in"), 16)
            act.wait_ge(sem("x_in"), 16)

            def norm(n):
                c0, layer, s2, cond = NORMS[n]
                T = s2 * SEQ
                for k in range(KD):
                    if n:
                        act.wait_ge(sem("res_done"), RB[RES[n - 1][0]] + (k + 1) * s2)
                    x = X[:, 0:s2 * 2048].rearrange("p (s k t) -> p k s t", k=KD, t=SEQ)[:, k]
                    act.activation(SQ[:, k * T:(k + 1) * T].rearrange("p (s t) -> p s t", t=SEQ), x, ACT.Square).then_inc(
                        sem("sq_done"), 1)
                act.wait_ge(sem("stat_done"), n + 1)
                act.activation(RN[:, 0:T], PS[:, 7, 0:T], ACT.Sqrt, bias=eps, scale=1.0 / D).then_inc(
                    sem("root_done"), 1)
                for k in range(KD):
                    for s in range(s2):
                        act.wait_ge(sem("scaled"), HB[n] + k * s2 + s + 1)
                        h = H[:, k * T + s * SEQ:k * T + (s + 1) * SEQ]
                        act.activation(h, h, ACT.Identity, bias=mod(layer, c0 + k, cond + s)).then_inc(
                            sem("h_ready"), 1)

            def ffn_in(l):
                T = 2 * SEQ if l == 0 else SEQ
                with act.Fori(0, 2) as it:
                    for s in range(11):
                        act.wait_ge(sem("product"), MMB[f"fin{l}"] + (it * 11 + (s + 1)))
                        b = s % 3
                        act.activation(ST3[:, b, 0:T], PS[:, 2 * b, 0:T], ACT.Silu).then_inc(sem("silu_done"), 1)

            def head_norm(i, bank):
                _, _, T = HN[i]
                if i < 16:
                    act.wait_ge(sem("hn_mm"), i + 1)
                elif i < 20:
                    act.wait_ge(sem("product"), MMB["win"] + (i - 16 + 5))
                else:
                    act.wait_ge(sem("hn_mm"), i - 4 + 1)
                if i >= 2:
                    act.wait_ge(sem("hn_done"), i - 1)
                act.activation(HSQ[:, i % 2, 0:T], PS[:, bank, 0:T], ACT.Square).then_inc(sem("hn_sq"), 1)

            def head_root(i, stat):
                _, _, T = HN[i]
                act.wait_ge(sem("hn_stat"), i + 1)
                is_q = i < 8 or 16 <= i < 20
                act.activation(HSQ[:, i % 2, 0:T], PS[:, stat, 0:T], ACT.Sqrt, bias=eps_q if is_q else eps,
                               scale=1.0 if is_q else 1.0 / HD).then_inc(sem("hn_root"), 1)

            def attention(a):
                t, n, u0 = a["tag"], a["n"], a["u0"]
                KT_ = a["kc"] * P

                def evict(u):
                    act.wait_ge(sem(f"tr_{t}"), u + 1)
                    if u >= 2:
                        act.wait_ge(sem(f"pv_{t}"), u - 1)
                    act.activation(a["pt"][:, u % 2, :], PS[:, 2 + u % 2, 0:KT_], ACT.Copy).then_inc(
                        sem(f"pt_{t}"), 1)

                for u in range(n):
                    act.wait_ge(sem(f"max_{t}"), u + 1)
                    if u >= 2:
                        act.wait_ge(sem(f"tr_{t}"), u - 1)
                    act.activation(a["p"][:, u % 2, :], PS[:, u % 2, 0:KT_], ACT.Exp, bias=NM[:, u % 2:u % 2 + 1],
                                   accum_out=SM[:, u % 2:u % 2 + 1]).then_inc(sem(f"exp_{t}"), 1)
                    if u >= 1:
                        evict(u - 1)
                evict(n - 1)

            def act_gathered():
                for t in range(2):
                    for b in range(4):
                        act.wait_ge(sem("pt_mm"), 4 * t + b + 1)
                        act.activation(PTS[:, 256 + b * 1024:256 + (b + 1) * 1024].rearrange(
                            "p (s k) -> p s k", k=SEQ)[:, :, t * P:(t + 1) * P],
                            PS[:, b, :].rearrange("p (s k) -> p s k", k=P), ACT.Copy).then_inc(sem("pts_copied"), 1)
                act.wait_ge(sem("gathered"), 1)
                act.activation(XG[:, 0:512], PS[:, 0, :], ACT.Copy).then_inc(sem("xg_act"), 1)
                with act.Fori(0, NE // 2) as it:
                    for e in range(2):
                        act.wait_ge(sem("gu_mm"), it * 8 + (4 * e + 4))
                        act.activation(SGF[:, e * 256:(e + 1) * 256].rearrange("p (q s) -> p q s", q=4),
                                       PS[:, e, :].rearrange("p (q g s) -> p q g s", q=4, g=2)[:, :, 0, :],
                                       ACT.Silu).then_inc(sem("m_silu"), 1)
                    act.wait_ge(sem("gathered"), it + 2)
                    act.activation(XG[:, 0:512], PS[:, 0, :], ACT.Copy).then_inc(sem("xg_act"), 1)
                    act.wait_ge(sem("dn_mm"), it * 2 + 3)
                    act.wait_ge(sem("scattered"), it + 1)
                    act.activation(YS[:, 0:512], PS[:, 2, :], ACT.Copy).then_inc(sem("ys_act"), 1)

            def act_dense():
                for b in range(16):
                    act.wait_ge(sem("cw_mm"), b + 1)
                    act.activation(CWB[:, b * 512:(b + 1) * 512], PS[:, b % 4, :], ACT.Copy).then_inc(sem("cw_copied"), 1)
                with act.Fori(0, NE // 2) as it:
                    for q in range(8):
                        act.wait_ge(sem("gu_mm"), it * 8 + (q + 1))
                        act.activation(SGM[:, (q % 4) * 256:(q % 4) * 256 + 256], PS[:, q % 4, 0:256], ACT.Silu).then_inc(
                            sem("m_silu"), 1)

            norm(0)
            for j in range(KD):
                act.wait_ge(sem("product"), MMB["conv"] + (j + 1))
                if j >= 2:
                    act.wait_ge(sem("conv_done"), j - 1)
                act.activation(CT[:, (j % 2) * 512:(j % 2) * 512 + 512], PS[:, 3 * (j % 2) + 1, :], ACT.Copy).then_inc(
                    sem("c_copied"), 1)
            norm(1)
            ffn_in(0)
            norm(2)
            for i in range(16):
                head_norm(i, i % 3)
                head_root(i, 3 + i % 2)
            for g in range(8):
                act.wait_ge(sem("v_mm"), g + 1)
                act.activation(V1[:, g % 4, (g // 4) * 512:(g // 4) * 512 + 512], PS[:, 5 + g % 3, :], ACT.Copy).then_inc(
                    sem("v_copied"), 1)
            attention(ATT[0])
            norm(3)
            ffn_in(1)
            norm(4)
            for i in range(24):
                if 4 <= i < 8:
                    head_norm(16 + i - 4, i % 4)
                    head_root(16 + i - 4, 4 + i % 2)
                    continue
                act.wait_ge(sem("product"), MMB["win"] + (i + 1))
                act.activation(WIN[i], PS[:, i % 4, 0:SEQ], ACT.Copy).then_inc(sem("win_copied"), 1)
                if i == 1:
                    act.wait_ge(sem("win_copied"), 2)
                    act.activation(LSQ, LATB, ACT.Square).then_inc(sem("lat_sq"), 1)
                if i == 13:
                    act.wait_ge(sem("lat_stat"), 1)
                    act.activation(RN[:, 0:SEQ], PS[:, 6, 0:SEQ], ACT.Sqrt, bias=eps, scale=1.0 / LAT).then_inc(
                        sem("lat_root"), 1)
            act.wait_ge(sem("wi_mm"), 1)
            act.activation(SC3[:, 0:16], PS[:, 6, 256:272], ACT.Copy, scale=1.0 / 16.0).then_inc(sem("wi_done"), 1)
            for i in range(4):
                head_norm(20 + i, i)
                head_root(20 + i, 4 + i % 2)
            for t in range(2):
                act.wait_ge(sem("va_mm"), t + 1)
                act.activation(VA[:, t, :], PS[:, 6 + t, :], ACT.Copy).then_inc(sem("va_copied"), 1)
            for v in range(16):
                h = v % 8
                act.wait_ge(sem("dots"), v + 1)
                if v >= 4:
                    act.wait_ge(sem("scored"), v - 3)
                act.activation(RL[:, v % 4, :], PS[:, 4 + h % 4, 0:256], ACT.Relu).then_inc(
                    sem("relu"), 1)
            attention(ATT[1])

            act.wait_ge(sem("mixed"), 5)
            act.activation(RP[0:64, 0:256], RP[0:64, 0:256], ACT.Tanh).then_inc(sem("lora_in"), 1)
            act.activation(RP[:, 256:768], RP[:, 256:768], ACT.Sigmoid).then_inc(sem("lora_in"), 1)
            act.wait_ge(sem("lora_z"), 1)
            for m in range(4):
                act.activation(WW[:, m * 256:(m + 1) * 256], PS[:, m // 2, (m % 2) * 256:(m % 2) * 256 + 256],
                               ACT.Sigmoid, bias=vec("w0", m, m + 1)).then_inc(sem("w_sig"), 1)
            act.wait_ge(sem("lora_a"), 1)
            for m in range(4):
                act.activation(AA[:, m * 256:(m + 1) * 256], PS[:, 2 + m // 2, (m % 2) * 256:(m % 2) * 256 + 256],
                               ACT.Sigmoid, bias=vec("a0", m, m + 1)).then_inc(sem("a_sig"), 1)
            act.wait_ge(sem("product"), MMB["lora"] + (1))
            act.activation(GG, ps2(4), ACT.Copy).then_inc(sem("g_copied"), 1)
            act.wait_ge(sem("kk_raw"), 1)
            act.activation(TS, KK, ACT.Square).then_inc(sem("kk_sq"), 1)
            act.wait_ge(sem("kk_stat"), 1)
            act.activation(RNK, ps2(0), ACT.Sqrt).then_inc(sem("kk_root"), 1)
            act.wait_ge(sem("cum"), 1)
            act.activation(WW, WW, ACT.Exp).then_inc(sem("exp_prev"), 1)
            act.activation(EE, LL, ACT.Exp).then_inc(sem("exp_cum"), 1)
            act.wait_ge(sem("used_cum"), 1)
            act.activation(EE, LL, ACT.Exp, scale=-1.0).then_inc(sem("exp_inv"), 1)
            for i, dst in enumerate((BT, KT, VT)):
                act.wait_ge(sem("tok_mm"), i + 1)
                act.activation(dst, ps2((0, 2, 4)[i]), ACT.Copy).then_inc(sem("tok_copied"), 1)
            for lv in range(6):
                for b in range(2):
                    act.wait_ge(sem("p1_mm"), 2 * lv + b + 1)
                    act.activation(PX[:, b * 512:(b + 1) * 512], PS[:, b, :], ACT.Copy).then_inc(sem("p1_copied"), 1)
            for c in range(NCH):
                act.wait_ge(sem("rhs_mm"), c + 1)
                act.activation(RHS, PS[:, 0, 0:256], ACT.Copy).then_inc(sem("rhs_copied"), 1)
                act.wait_ge(sem("sa_mm"), c + 1)
                if c:
                    act.wait_ge(sem("y_mm"), c)
                act.activation(SA, PS[:, 1, 0:256], ACT.Copy, scale=-1.0).then_inc(sem("sa_copied"), 1)
            act.wait_ge(sem("y_mm"), NCH)
            act.activation(YY, ps2(6), ACT.Copy).then_inc(sem("y_copied"), 1)
            act.wait_ge(sem("centred"), 1)
            act.activation(TI, YY, ACT.Square).then_inc(sem("var_sq"), 1)
            act.wait_ge(sem("var_stat"), 1)
            act.activation(TIT, ps2(2), ACT.Sqrt, bias=gn_eps, scale=1.0 / HD).then_inc(sem("var_root"), 1)
            for m in range(KD):
                act.wait_ge(sem("product"), MMB["gates"] + (m + 1))
                if m >= 2:
                    act.wait_ge(sem("merged"), m - 1)
                act.activation(SG[:, m % 2, :], PS[:, 2 * (m % 2), :], ACT.Sigmoid).then_inc(sem("gate_sig"), 1)
            norm(5)
            for b in range(4):
                act.wait_ge(sem("xt_mm"), b + 1)
                act.activation(XT[:, b // 2, (b % 2) * 512:(b % 2) * 512 + 512], PS[:, b, :], ACT.Copy).then_inc(
                    sem("xt_copied"), 1)
            act.wait_ge(sem("g_shift"), 1)
            act.activation(RT[:, 0:8], RT[:, 0:8], ACT.Exp).then_inc(sem("g_exp"), 1)
            act.wait_ge(sem("e_diff"), 1)
            act.activation(RT[:, 8:10], RT[:, 8:10], ACT.Exp).then_inc(sem("e_exp"), 1)
            busiest = count_of(act)
            with act.If(busiest < CAP + 1):
                act_gathered()
            with act.Else():
                act_dense()

        @block.tensor
        def _(pe):
            pe.wait_ge(sem("cond"), 1)
            pe.wait_ge(sem("consts_in"), 16)

            def ada_first():
                slot_landed(pe, "ada0", 0)
                for m in range(4):
                    if m == 2:
                        ada_sum(0, 1)
                    for k in range(KD):
                        mm = pe.matmul(PS[:, 6, m * 2:m * 2 + 2], slot("ada0", 0, k * GRP + m * P, k * GRP + m * P + P),
                                       CS[:, 3 * k:3 * k + 2], start=(k == 0), stop=(k == KD - 1))
                mm.then_inc(sem("product"), 1)
                ada_sum(0, 2)

            def ada_sum(l, g, it=0, per_turn=0):
                conds = 1 if l == 2 else 2
                n = g + PG_BASE[l] - (PE_G if l == 0 else 0)
                done = 2 * KD * min(n, PG_BASE[2]) + KD * max(n - PG_BASE[2], 0)
                pe.wait_ge(sem("ada_step"), it * (per_turn * KD * conds) + (done + KD * conds))
                for m in range(4):
                    for c in range(conds):
                        col = (g * 4 + m) * 2 + (1 if l == 2 else c)
                        col = bass.ds(it * (8 * per_turn) + col, 1) if per_turn else slice(col, col + 1)
                        mm = pe.matmul(PS[:, 6, col], ACC[:, c, m * P:(m + 1) * P], ones[:, 0:1], start=True, stop=True)
                mm.then_inc(sem("ada_mm"), 1)

            def norm(n):
                T = NORMS[n][2] * SEQ
                for k in range(KD):
                    pe.wait_ge(sem("sq_done"), 8 * n + k + 1)
                    mm = pe.matmul(PS[:, 7, 0:T], ones, SQ[:, k * T:(k + 1) * T], start=(k == 0), stop=(k == KD - 1))
                mm.then_inc(sem("stat_done"), 1)

            def h_wait(n, k):
                pe.wait_ge(sem("h_ready"), HB[n] + (k + 1) * NORMS[n][2])

            def ffn(l):
                T = 2 * SEQ if l == 0 else SEQ
                stage = f"fin{l}"
                with pe.Fori(0, 2) as it:
                    for s in range(11):
                        slot_landed(pe, stage, s, it)
                        pe.wait_ge(sem("hid_done"), it * 11 + (s + (1 if s < 2 else 0)) + 22 * l)
                        for half in range(2):
                            for k in range(KD):
                                if s == 0 and half == 0:
                                    h_wait(2 * l + 1, k)
                                mm = pe.matmul(PS[:, 2 * (s % 3) + half, 0:T],
                                               slot(stage, s, k * 256 + half * 128, k * 256 + half * 128 + 128),
                                               h_of(k, T), start=(k == 0), stop=(k == KD - 1))
                        mm.then_inc(sem("product"), 1)
                        if s in (1, 3, 5, 7, 9):
                            ada_sum(l + 1, s // 2, it, 5)
                pe.wait_ge(sem("hid_done"), 22 * (l + 1) + 2)
                stage = f"fout{l}"
                s2 = T // SEQ
                with pe.Fori(0, 2) as it:
                    for s in range(4):
                        if s == 2:
                            ada_sum(l + 1, 10, it, 1)
                        slot_landed(pe, stage, s, it)
                        pe.wait_ge(sem("res_done"), it * 4 * s2 + (RB[stage] + (s - 3) * s2))
                        for k in range(KF):
                            mm = pe.matmul(PS[:, s, 0:T], slot(stage, s, k * 128, k * 128 + 128),
                                           HID[:, k * T:(k + 1) * T], start=(k == 0), stop=(k == KF - 1))
                        mm.then_inc(sem("product"), 1)

            def out_proj(stage, rhs_of, T):
                s2 = T // SEQ
                for m in range(KD):
                    if m % 4 == 0:
                        slot_landed(pe, stage, m // 4)
                    if m >= 4:
                        pe.wait_ge(sem("res_done"), RB[stage] + (m - 3) * s2)
                    for k in range(KD):
                        mm = pe.matmul(PS[:, m % 4, 0:T],
                                       slot(stage, m // 4, k * 512 + (m % 4) * 128, k * 512 + (m % 4) * 128 + 128),
                                       rhs_of(k), start=(k == 0), stop=(k == KD - 1))
                    mm.then_inc(sem("product"), 1)
                    if stage == "cout" and m == 1:
                        ada_sum(0, 11)

            def head_stat(i, stat):
                T = HN[i][2]
                pe.wait_ge(sem("hn_sq"), i + 1)
                pe.matmul(PS[:, stat, 0:T], bo64, HSQ[:, i % 2, 0:T], start=True, stop=True).then_inc(sem("hn_stat"), 1)

            def attention(a):
                t, n, KC = a["tag"], a["n"], a["kc"]

                def scores(u):
                    h, tt = divmod(u, 2)
                    r = 64 * (h % 2)
                    if a["bias"] is not None:
                        pe.wait_ge(sem("bias_made"), u + 1)
                    if u >= 2:
                        pe.wait_ge(sem(f"exp_{t}"), u - 1)
                    pe.matmul(PS[:, u % 2, 0:KC * P], a["q"][r:r + 64, h // 2, tt * P:(tt + 1) * P],
                              a["k"][r:r + 64, h // 2, 0:KC * P], start=True, stop=False)
                    pe.matmul(PS[:, u % 2, 0:256], ident, bias_of(a, u), start=False, stop=True).then_inc(
                        sem(f"s_{t}"), 1)

                def turn(u):
                    pe.wait_ge(sem(f"p_{t}"), u + 1)
                    if u >= 2:
                        pe.wait_ge(sem(f"pt_{t}"), u - 1)
                    for kc in range(KC):
                        mm = pe.transpose(PS[:, 2 + u % 2, kc * P:(kc + 1) * P], a["p"][:, u % 2, kc * P:(kc + 1) * P],
                                          ident)
                    mm.then_inc(sem(f"tr_{t}"), 1)

                def pv(u):
                    h, tt = divmod(u, 2)
                    hp = h // 2
                    r = 64 * (h % 2)
                    pe.wait_ge(sem(f"pt_{t}"), u + 1)
                    if u % 4 == 0 and hp >= 2:
                        pe.wait_ge(sem(f"o_{t}"), hp - 1)
                    for kc in range(KC):
                        mm = pe.matmul(PS[r:r + 64, 4 + hp % 2, tt * P:(tt + 1) * P], a["v"][:, kc, h * 64:(h + 1) * 64],
                                       a["pt"][:, u % 2, kc * P:(kc + 1) * P], start=(kc == 0), stop=(kc == KC - 1))
                    mm.then_inc(sem(f"pv_{t}"), 1)

                scores(0)
                for u in range(n):
                    if u + 1 < n:
                        scores(u + 1)
                    turn(u)
                    if u >= 1:
                        pv(u - 1)
                pv(n - 1)

            def pe_gathered():
                def gather(p):
                    for c in range(KD):
                        for t in range(2):
                            mm = pe.matmul(PS[:, c // 4, (c % 4) * P:(c % 4) * P + P], XT[:, t, c * P:(c + 1) * P],
                                           PG[:, t, bass.ds(p * P, P)] if not isinstance(p, int) else PG[:, t, p * P:p * P + P],
                                           start=(t == 0), stop=(t == 1))
                    mm.then_inc(sem("gathered"), 1)

                def scatter(p):
                    rhs = PTS[:, bass.ds(p * SEQ, SEQ)] if not isinstance(p, int) else PTS[:, p * SEQ:(p + 1) * SEQ]
                    for m in range(KD):
                        mm = pe.matmul(PS[:, 4 + m // 2, (m % 2) * SEQ:(m % 2 + 1) * SEQ], YS[:, m * P:(m + 1) * P], rhs,
                                       start=False, stop=False, skip_group_check=True)
                    mm.then_inc(sem("scattered"), 1)

                pe.wait_ge(sem("zeros"), 1)
                for b in range(4):
                    pe.matmul(PS[:, 4 + b, :], ident, CT0, start=True, stop=True)
                for t in range(2):
                    pe.wait_ge(sem("pcw_made"), t + 1)
                    for b in range(4):
                        if t:
                            pe.wait_ge(sem("pts_copied"), b + 1)
                        for s in range(4):
                            mm = pe.transpose(PS[:, b, s * P:(s + 1) * P], PCW[:, (4 * b + s) * P:(4 * b + s + 1) * P], ident)
                        mm.then_inc(sem("pt_mm"), 1)
                pe.wait_ge(sem("pts_copied"), 8)
                pe.wait_ge(sem("xt_copied"), 4)
                gather(0)
                with pe.Fori(0, NE // 2) as it:
                    def gate_up(e):
                        for q in range(4):
                            s = 2 * e + q // 2
                            if q % 2 == 0:
                                slot_landed(pe, "moe", s, it)
                            for g in range(2):
                                for k in range(KD):
                                    w = k * 512 + (2 * (q % 2) + g) * P
                                    mm = pe.matmul(PS[:, e, (2 * q + g) * CAP:(2 * q + g + 1) * CAP], slot("moe", s, w, w + P),
                                                   XG[:, k * P + e * CAP:k * P + (e + 1) * CAP],
                                                   start=(k == 0), stop=(k == KD - 1))
                            mm.then_inc(sem("gu_mm"), 1)

                    def down(e):
                        slot_landed(pe, "moe", 4 + e, it)
                        pe.wait_ge(sem("hf_done"), it * 2 + (e + 1))
                        for half in range(2):
                            for q in range(4):
                                w = q * D + half * 512
                                mm = pe.matmul(PS[CAP * e:CAP * (e + 1), 2 + half, :],
                                               HF[:, e * 256 + q * CAP:e * 256 + (q + 1) * CAP],
                                               slot("moe", 4 + e, w, w + 512), start=(q == 0), stop=(q == 3))
                        mm.then_inc(sem("dn_mm"), 1)

                    pe.wait_ge(sem("xg_act"), it + 1)
                    pe.wait_ge(sem("xg_dve"), it + 1)
                    gate_up(0)
                    pe.wait_ge(sem("ys_act"), it + 1)
                    pe.wait_ge(sem("ys_dve"), it + 1)
                    scatter(it)
                    gate_up(1)
                    down(0)
                    pe.wait_ge(sem("hf_done"), it * 2 + 2)
                    gather(it + 1)
                    down(1)
                pe.wait_ge(sem("ys_act"), NE // 2 + 1)
                pe.wait_ge(sem("ys_dve"), NE // 2 + 1)
                scatter(NE // 2)

            def pe_dense():
                pe.wait_ge(sem("combined"), 1)
                for t in range(2):
                    mm = pe.transpose(PS[0:NE, 5, t * P:(t + 1) * P], CMB[:, t, :], ident)
                mm.then_inc(sem("cmb_mm"), 1)
                pe.wait_ge(sem("cmb_copied"), 1)
                for e in range(NE):
                    if e % 2 == 0 and e >= 8:
                        pe.wait_ge(sem("cw_copied"), e // 2 - 3)
                    mm = pe.matmul(PS[:, (e // 2) % 4, (e % 2) * 256:(e % 2) * 256 + 256],
                                   ident[0:NE, e:e + 1].to_broadcast([NE, P]), CTB, start=True, stop=True)
                    if e % 2:
                        mm.then_inc(sem("cw_mm"), 1)
                pe.wait_ge(sem("cw_copied"), 16)
                pe.wait_ge(sem("zeros"), 1)
                for b in range(4):
                    pe.matmul(PS[:, 4 + b, :], ident, CT0, start=True, stop=True)
                with pe.Fori(0, NE // 2) as it:
                    def gate_up(e, q):
                        s = 2 * e + q // 2
                        if q % 2 == 0:
                            slot_landed(pe, "moe", s, it)
                        pe.wait_ge(sem("hm_done"), it * 8 + (4 * e + q + 1))
                        for g in range(2):
                            for k in range(KD):
                                w = k * 512 + (2 * (q % 2) + g) * 128
                                mm = pe.matmul(PS[:, q, g * 256:g * 256 + 256], slot("moe", s, w, w + 128),
                                               XN[:, k * SEQ:(k + 1) * SEQ], start=(k == 0), stop=(k == KD - 1))
                        mm.then_inc(sem("gu_mm"), 1)

                    def down(e):
                        slot_landed(pe, "moe", 4 + e, it)
                        for m in range(KD):
                            for q in range(4):
                                if m == 0:
                                    pe.wait_ge(sem("hm_done"), it * 8 + (4 * e + q + 5))
                                mm = pe.matmul(PS[:, 4 + m // 2, (m % 2) * 256:(m % 2) * 256 + 256],
                                               slot("moe", 4 + e, q * 1024 + m * 128, q * 1024 + m * 128 + 128),
                                               HM[:, e * 1024 + q * 256:e * 1024 + q * 256 + 256],
                                               start=False, stop=False, skip_group_check=True)
                        return mm

                    for e in range(2):
                        for q in range(4):
                            gate_up(e, q)
                        down(e).then_inc(sem("dn_mm"), 1)

            ada_first()
            norm(0)
            ada_sum(0, 3)
            for j in range(KD):
                slot_landed(pe, "conv", j)
                if j >= 2:
                    pe.wait_ge(sem("conv_done"), j - 1)
                for c in range(3):
                    for k in range(KD):
                        if j == 0 and c == 0:
                            h_wait(0, k)
                        mm = pe.matmul(PS[:, 3 * (j % 2) + c, :], slot("conv", j, k * 384 + c * 128, k * 384 + c * 128 + 128),
                                       h_of(k, 512), start=(k == 0), stop=(k == KD - 1))
                mm.then_inc(sem("product"), 1)
                if j:
                    ada_sum(0, 3 + j)
            pe.wait_ge(sem("conv_done"), KD)
            out_proj("cout", lambda k: YC[:, k * 512:(k + 1) * 512], 512)
            norm(1)
            ffn(0)
            norm(2)
            for i in range(16):
                if i % 4 == 0:
                    slot_landed(pe, "qkv", i // 4)
                if i >= 3:
                    pe.wait_ge(sem("hn_done"), i - 2)
                T = HN[i][2]
                for k in range(KD):
                    if i == 0:
                        h_wait(2, k)
                    mm = pe.matmul(PS[:, i % 3, 0:T],
                                   slot("qkv", i // 4, k * 512 + (i % 4) * 128, k * 512 + (i % 4) * 128 + 128),
                                   h_of(k, 512)[:, 0:T], start=(k == 0), stop=(k == KD - 1))
                mm.then_inc(sem("hn_mm"), 1)
                if i >= 1:
                    head_stat(i - 1, 3 + (i - 1) % 2)
            for g in range(8):
                if g % 4 == 0:
                    slot_landed(pe, "qkv", 4 + g // 4)
                if g >= 3:
                    pe.wait_ge(sem("v_copied"), g - 2)
                for k in range(KD):
                    mm = pe.matmul(PS[:, 5 + g % 3, :], h_of(k, 512)[:, (g % 4) * P:(g % 4 + 1) * P],
                                   slot("qkv", 4 + g // 4, k * 512, k * 512 + 512), start=(k == 0), stop=(k == KD - 1))
                mm.then_inc(sem("v_mm"), 1)
                if g == 0:
                    head_stat(15, 3 + 1)
            pe.wait_ge(sem("v_copied"), 8)
            pe.wait_ge(sem("hn_done"), 16)
            pe.wait_ge(sem("bias_in"), 1)
            attention(ATT[0])
            pe.wait_ge(sem("o_na"), 8)
            out_proj("aout", lambda k: O1[:, k * SEQ:(k + 1) * SEQ], SEQ)
            norm(3)
            ffn(1)
            norm(4)
            for i in range(24):
                if i % 4 == 0:
                    slot_landed(pe, "win", i // 4)
                if i >= 4:
                    if 8 <= i < 12:
                        pe.wait_ge(sem("hn_done"), 16 + i - 7)
                    else:
                        pe.wait_ge(sem("win_copied"), sum(c <= i - 4 for c in COPIES))
                for k in range(KD):
                    if i == 0:
                        h_wait(4, k)
                    mm = pe.matmul(PS[:, i % 4, 0:SEQ],
                                   slot("win", i // 4, k * 512 + (i % 4) * 128, k * 512 + (i % 4) * 128 + 128),
                                   XN[:, k * SEQ:(k + 1) * SEQ], start=(k == 0), stop=(k == KD - 1))
                mm.then_inc(sem("product"), 1)
                if 5 <= i < 9:
                    head_stat(16 + i - 5, 4 + (i - 5) % 2)
                if i == 10:
                    pe.wait_ge(sem("lat_sq"), 1)
                    for c in range(2):
                        mm = pe.matmul(PS[:, 6, 0:SEQ], ones, LSQ[:, c * SEQ:(c + 1) * SEQ], start=(c == 0), stop=(c == 1))
                    mm.then_inc(sem("lat_stat"), 1)
                if i == 14:
                    pe.wait_ge(sem("lat_root"), 1)
                    for t in range(2):
                        for k in range(KD):
                            mm = pe.matmul(PS[:, 6, 256 + t * 8:264 + t * 8], XN[:, k * SEQ + t * P:k * SEQ + (t + 1) * P],
                                           vec("w_i", k * 8, k * 8 + 8), start=(k == 0), stop=(k == KD - 1))
                    mm.then_inc(sem("wi_mm"), 1)
            slot_landed(pe, "kvup", 0)
            pe.wait_ge(sem("lat_done"), 2)
            pe.wait_ge(sem("win_copied"), len(COPIES))
            pe.wait_ge(sem("hn_done"), 20)
            for i in range(4):
                for k in range(2):
                    mm = pe.matmul(PS[:, i, 0:SEQ], slot("kvup", 0, k * 1024 + i * 128, k * 1024 + i * 128 + 128),
                                   LATB[:, k * SEQ:(k + 1) * SEQ], start=(k == 0), stop=(k == 1))
                mm.then_inc(sem("hn_mm"), 1)
            for i in range(2):
                head_stat(20 + i, 4 + i)
            pe.wait_ge(sem("wi_done"), 1)
            for t in range(2):
                for k in range(2):
                    mm = pe.matmul(PS[:, 6 + t, :], LATB[:, k * SEQ + t * P:k * SEQ + (t + 1) * P],
                                   slot("kvup", 0, k * 1024 + 512, k * 1024 + 1024), start=(k == 0), stop=(k == 1))
                mm.then_inc(sem("va_mm"), 1)
            for i in range(2, 4):
                head_stat(20 + i, 4 + i % 2)
            pe.wait_ge(sem("va_copied"), 2)
            pe.wait_ge(sem("hn_done"), 24)
            for v in range(16):
                t, h = divmod(v, 8)
                r = 32 * (h % 4)
                if v >= 4:
                    pe.wait_ge(sem("relu"), v - 3)
                pe.matmul(PS[:, 4 + h % 4, 0:256], QI[r:r + 32, h // 4, t * P:(t + 1) * P],
                          KI[r:r + 32, :], start=True, stop=True, tile_position=(r, 0)).then_inc(sem("dots"), 1)
                if v == 15:
                    pe.wait_ge(sem("relu"), 16)
            attention(ATT[1])

            slot_landed(pe, "lora", 0)
            pe.wait_ge(sem("lora_in"), 2)
            pe.wait_ge(sem("o_dsa"), 4)
            for m in range(4):
                mm = pe.matmul(PS[:, m // 2, (m % 2) * 256:(m % 2) * 256 + 256], slot("lora", 0, m * 128, m * 128 + 128, 0, 64),
                               RP[0:64, 0:256], start=True, stop=True)
            mm.then_inc(sem("lora_z"), 1)
            for m in range(4):
                mm = pe.matmul(PS[:, 2 + m // 2, (m % 2) * 256:(m % 2) * 256 + 256],
                               slot("lora", 0, m * 128, m * 128 + 128, 64, 128), RP[64:128, 0:256], start=True, stop=True)
            mm.then_inc(sem("lora_a"), 1)
            for m in range(4):
                dst = PS[:, 4 + m // 2, (m % 2) * 256:(m % 2) * 256 + 256]
                pe.matmul(dst, slot("lora", 0, 512 + m * 128, 640 + m * 128), RP[:, 256:512], start=True, stop=False)
                mm = pe.matmul(dst, slot("lora", 0, 1024 + m * 128, 1152 + m * 128), RP[:, 512:768], start=False, stop=True)
            mm.then_inc(sem("product"), 1)
            pe.wait_ge(sem("kk_sq"), 1)
            for b in range(2):
                mm = pe.matmul(PS[:, b, :], bo64, TS[:, b * 512:(b + 1) * 512], start=True, stop=True)
            mm.then_inc(sem("kk_stat"), 1)
            pe.wait_ge(sem("rk_made"), 1)
            for b in range(2):
                mm = pe.matmul(PS[:, 2 + b, :], bo64, EE[:, b * 512:(b + 1) * 512], start=True, stop=True)
            mm.then_inc(sem("rk_sum"), 1)
            for i, (src, ready) in enumerate(((BB, "b_hat"), (RK, "k_hat"), (RV, "k_hat"))):
                pe.wait_ge(sem(ready), 1)
                for c in range(NCH):
                    for hp in range(HP):
                        for h in range(2):
                            b = 2 * i + c // 2
                            o = ((c % 2) * HP + hp) * 64
                            mm = pe.matmul(PS[64 * h:64 * h + 64, b, o:o + 64], f64(src, c, hp, h),
                                           con("id64")[64 * h:64 * h + 64, :], start=True, stop=True)
                mm.then_inc(sem("tok_mm"), 1)
            for i, (left, right) in enumerate(((BB, KK), (RK, KK), (BB, RR), (RK, RR))):
                b0 = (6, 0, 2, 4)[i]
                if i:
                    pe.wait_ge(sem("tok_copied"), i)
                for c in range(NCH):
                    for hp in range(HP):
                        for h in range(2):
                            b = b0 + c // 2
                            o = ((c % 2) * HP + hp) * 64
                            mm = pe.matmul(PS[64 * h:64 * h + 64, b, o:o + 64], f64(left, c, hp, h),
                                           f64(right, c, hp, h), start=True, stop=True)
                mm.then_inc(sem("tri_mm"), 1)
            for lv in range(6):
                if lv == 0:
                    pe.wait_ge(sem("tri_masked"), 8)
                for b in range(2):
                    pe.wait_ge(sem("lv_masked"), lv + 1)
                    for c in range(2 * b, 2 * b + 2):
                        for hp in range(HP):
                            for h in range(2):
                                o = ((c % 2) * HP + hp) * 64
                                mm = pe.matmul(PS[64 * h:64 * h + 64, b, o:o + 64], c64(MX, c, hp, h),
                                               c64(TI, c, hp, h), start=True, stop=True)
                    mm.then_inc(sem("p1_mm"), 1)
                for b in range(2):
                    pe.wait_ge(sem("p1_copied"), 2 * lv + b + 1)
                    for c in range(2 * b, 2 * b + 2):
                        for hp in range(HP):
                            for h in range(2):
                                o = ((c % 2) * HP + hp) * 64
                                pe.matmul(PS[64 * h:64 * h + 64, 2 + b, o:o + 64], c64(TIT, c, hp, h),
                                          c64(PX, c, hp, h), start=True, stop=True)
                                mm = pe.matmul(PS[64 * h:64 * h + 64, 4 + b, o:o + 64], c64(PX, c, hp, h),
                                               c64(TIT, c, hp, h), start=True, stop=True)
                    mm.then_inc(sem("p2_mm"), 1)
            pe.wait_ge(sem("t_done"), 24)
            for c in range(NCH):
                st = ST[:, (c % 2) * 256:(c % 2) * 256 + 256]
                if c:
                    pe.wait_ge(sem("state"), c)
                for hp in range(HP):
                    for h in range(2):
                        dst = PS[64 * h:64 * h + 64, 0, hp * 64:hp * 64 + 64]
                        if c:
                            pe.matmul(dst, f64(KK, c, hp, h), st[64 * h:64 * h + 64, hp * 64:hp * 64 + 64],
                                      start=True, stop=False)
                        mm = pe.matmul(dst, c64(AKT, c, hp, h), c64(VT, c, hp, h), start=(c == 0), stop=True)
                mm.then_inc(sem("rhs_mm"), 1)
                pe.wait_ge(sem("rhs_copied"), c + 1)
                for hp in range(HP):
                    for h in range(2):
                        mm = pe.matmul(PS[64 * h:64 * h + 64, 1, hp * 64:hp * 64 + 64], c64(TIT, c, hp, h),
                                       RHS[64 * h:64 * h + 64, hp * 64:hp * 64 + 64], start=True, stop=True)
                mm.then_inc(sem("sa_mm"), 1)
                pe.wait_ge(sem("sa_copied"), c + 1)
                for hp in range(HP):
                    for h in range(2):
                        dst = PS[64 * h:64 * h + 64, 2, hp * 64:hp * 64 + 64]
                        pe.matmul(dst, c64(BT, c, hp, h), SA[64 * h:64 * h + 64, hp * 64:hp * 64 + 64],
                                  start=True, stop=False)
                        mm = pe.matmul(dst, c64(KT, c, hp, h), c64(VT, c, hp, h), start=False, stop=True)
                mm.then_inc(sem("state_mm"), 1)
                for hp in range(HP):
                    for h in range(2):
                        o = (hp % 2) * 256 + c * CH
                        dst = PS[64 * h:64 * h + 64, 6 + hp // 2, o:o + CH]
                        if c:
                            pe.matmul(dst, st[64 * h:64 * h + 64, hp * 64:hp * 64 + 64], f64(RR, c, hp, h),
                                      start=True, stop=False)
                        pe.matmul(dst, SA[64 * h:64 * h + 64, hp * 64:hp * 64 + 64], c64(RBT, c, hp, h),
                                  start=(c == 0), stop=False)
                        mm = pe.matmul(dst, c64(VT, c, hp, h), c64(RKT, c, hp, h), start=False, stop=True)
                mm.then_inc(sem("y_mm"), 1)
            pe.wait_ge(sem("y_copied"), 1)
            for b in range(2):
                mm = pe.matmul(PS[:, b, :], bo64, YY[:, b * 512:(b + 1) * 512], start=True, stop=True)
            mm.then_inc(sem("mean_sum"), 1)
            pe.wait_ge(sem("var_sq"), 1)
            pe.wait_ge(sem("state"), NCH)
            for b in range(2):
                mm = pe.matmul(PS[:, 2 + b, :], bo64, TI[:, b * 512:(b + 1) * 512], start=True, stop=True)
            mm.then_inc(sem("var_stat"), 1)
            pe.wait_ge(sem("o_rwkv"), 1)
            for m in range(KD):
                slot_landed(pe, "gates", m)
                if m >= 2:
                    pe.wait_ge(sem("merged"), m - 1)
                b = 2 * (m % 2)
                for g in range(2):
                    for k in range(KD):
                        pe.matmul(PS[:, b, g * 256:g * 256 + 256], slot("gates", m, g * 1024 + k * 128, g * 1024 + k * 128 + 128),
                                  XN[:, k * SEQ:(k + 1) * SEQ], start=(k == 0), stop=(k == KD - 1))
                for g, o in enumerate((OA, YY)):
                    for k in range(4):
                        w = 2048 + g * 512 + k * 128
                        mm = pe.matmul(PS[:, b + 1, g * 256:g * 256 + 256], slot("gates", m, w, w + 128),
                                       o[:, k * SEQ:(k + 1) * SEQ], start=(k == 0), stop=(k == 3))
                mm.then_inc(sem("product"), 1)
            pe.wait_ge(sem("merged"), KD)
            out_proj("wout", lambda k: MG[:, k * SEQ:(k + 1) * SEQ], SEQ)
            norm(5)
            for k in range(KD):
                h_wait(5, k)
            pe.wait_ge(sem("root_done"), 6)
            for t in range(2):
                for k in range(KD):
                    mm = pe.matmul(PS[:, 6, t * 64:t * 64 + 36], XN[:, k * SEQ + t * P:k * SEQ + (t + 1) * P],
                                   vec("router", k * 36, k * 36 + 36), start=(k == 0), stop=(k == KD - 1))
            mm.then_inc(sem("logits"), 1)
            for b in range(4):
                for c in range(4):
                    mm = pe.transpose(PS[:, b, c * P:(c + 1) * P],
                                      XN[:, ((b % 2) * 4 + c) * SEQ + (b // 2) * P:((b % 2) * 4 + c) * SEQ + (b // 2) * P + P],
                                      ident)
                mm.then_inc(sem("xt_mm"), 1)
            pe.wait_ge(sem("indicated"), 1)
            pe.wait_ge(sem("rank_in"), 16)
            pe.matmul(PS[:, 6, 0:NE], UPPER, IND[:, 0, :], start=True, stop=True)
            pe.matmul(PS[:, 6, NE:2 * NE], ones, IND[:, 0, :], start=True, stop=False)
            pe.matmul(PS[:, 6, NE:2 * NE], UPPER, IND[:, 1, :], start=False, stop=True)
            pe.matmul(PS[:, 6, 2 * NE:3 * NE], ones, IND[:, 0, :], start=True, stop=False)
            pe.matmul(PS[:, 6, 2 * NE:3 * NE], ones, IND[:, 1, :], start=False, stop=True).then_inc(sem("ranked"), 1)
            busiest = count_of(pe)
            with pe.If(busiest < CAP + 1):
                pe_gathered()
            with pe.Else():
                pe_dense()

        @block.vector
        def _(dve):
            cnt = [0]

            def link(ins):
                cnt[0] += 1
                ins.then_inc(sem("dve_step"), 1)
                dve.wait_ge(sem("dve_step"), cnt[0])

            dve.wait_ge(sem("vecs_in"), 16)
            dve.wait_ge(sem("consts_in"), 16)
            dve.wait_ge(sem("cond"), 1)
            dve.memset(SC3[:, 0:1], 0.0).then_inc(sem("hid_done"), 2)
            dve.memset(SC3[:, 1:2], 0.0).then_inc(sem("hm_done"), 4)
            dve.memset(SC3[:, 2:3], 0.0).then_inc(sem("ada_mm"), 1)
            dve.memset(SC3[:, 3:4], 0.0).then_inc(sem("dn_mm"), 1)

            def ada_group(l, g, it=0, per_turn=0):
                cs = (2,) if l == 2 else (0, 1)
                conds = len(cs)
                n = g + PG_BASE[l] - (PE_G if l == 0 else 0)
                done = 2 * KD * min(n, PG_BASE[2]) + KD * max(n - PG_BASE[2], 0)
                dve.wait_ge(sem("ada_mm"), it * per_turn + (n + 1))
                for k in range(KD):
                    if k % 2 == 0:
                        dve.wait_ge(sem(f"ada_in{k // 2}"), it * (16 * per_turn) + 16 * (n + 1))
                    for i, c in enumerate(cs):
                        w = ADA[k // 2][:, (k % 2) * GRP:(k % 2 + 1) * GRP]
                        scale = CS[:, 3 * k + c:3 * k + c + 1]
                        if k == 0:
                            ins = dve.tensor_scalar(ACC[:, i, :], w, scale, None, ALU.mult)
                        else:
                            dve.wait_ge(sem("ada_step"), it * (per_turn * KD * conds) + (done + (k - 1) * conds + i + 1))
                            ins = dve.scalar_tensor_tensor(out=ACC[:, i, :], in0=w, scalar=scale, in1=ACC[:, i, :],
                                                           op0=ALU.mult, op1=ALU.add)
                        ins.then_inc(sem("ada_step"), 1)

            def ada(l, a, b, norms):
                if a == 0 and l == 0:
                    dve.wait_ge(sem("product"), MMB["ada0"] + PE_G)
                dve.wait_ge(sem("ada_mm"), PG_BASE[l] + b // 4 - (PE_G if l == 0 else 0) + 1)
                c, w = (1, 1) if l == 2 else (0, 2)
                m3 = MOD[:, l * 96 + 2 * a:l * 96 + 2 * b].rearrange("p (m c) -> p m c", c=2)[:, :, c:c + w]
                link(dve.tensor_tensor(m3, PS[:, 6, 2 * a:2 * b].rearrange("p (m c) -> p m c", c=2)[:, :, c:c + w],
                                       vec("b_ada", l * 48 + a, l * 48 + b).unsqueeze(2).to_broadcast([P, b - a, w]), ALU.add))
                for n in norms:
                    link(dve.scalar_tensor_tensor(
                        out=AB[:, n * 16:n * 16 + 16].rearrange("p (k c) -> p k c", c=2)[:, :, c:c + w],
                        in0=mod2(l, NORMS[n][0] + 8)[:, :, c:c + w], scalar=1.0,
                        in1=vec("g_norm", n * 8, n * 8 + 8).unsqueeze(2).to_broadcast([P, 8, w]), op0=ALU.add, op1=ALU.mult))

            def norm_root(n):
                T = NORMS[n][2] * SEQ
                dve.wait_ge(sem("root_done"), n + 1)
                link(dve.reciprocal(RN[:, 0:T], RN[:, 0:T]))

            def norm(n):
                _, _, s2, cond = NORMS[n]
                T = s2 * SEQ
                if n:
                    norm_root(n)
                for k in range(KD):
                    for s in range(s2):
                        a = n * 16 + 2 * k + cond + s
                        dve.scalar_tensor_tensor(out=H[:, k * T + s * SEQ:k * T + (s + 1) * SEQ],
                                                 in0=X[:, s * 2048 + k * SEQ:s * 2048 + (k + 1) * SEQ], scalar=AB[:, a:a + 1],
                                                 in1=RN[:, s * SEQ:(s + 1) * SEQ], op0=ALU.mult, op1=ALU.mult).then_inc(
                            sem("scaled"), 1)

            def residual(i):
                stage, c0, layer, s2 = RES[i]
                for m in range(KD):
                    if stage in ("fout0", "fout1") and m in (0, 4):
                        ada_group(layer + 1, 10 + m // 4)
                    if stage in ("fout0", "fout1") and m == 6:
                        ada(layer + 1, 0, 48, (2 * layer + 2, 2 * layer + 3))
                    dve.wait_ge(sem("product"), MMB[stage] + (m + 1))
                    for s in range(s2):
                        xs = X[:, s * 2048 + m * SEQ:s * 2048 + (m + 1) * SEQ]
                        dve.scalar_tensor_tensor(out=xs, in0=PS[:, m % 4, s * SEQ:(s + 1) * SEQ],
                                                 scalar=mod(layer, c0 + m, (1 if layer == 2 else 0) + s), in1=xs,
                                                 op0=ALU.mult, op1=ALU.add).then_inc(sem("res_done"), 1)

            def ffn_in(l):
                T = 2 * SEQ if l == 0 else SEQ
                with dve.Fori(0, 2) as it:
                    for s in range(11):
                        dve.wait_ge(sem("silu_done"), it * 11 + (22 * l + s + 1))
                        b = s % 3
                        dve.tensor_tensor(HID[:, bass.ds((it * 11 + s) * T, T)], ST3[:, b, 0:T], PS[:, 2 * b + 1, 0:T],
                                          ALU.mult).then_inc(sem("hid_done"), 1)
                        if s in (0, 2, 4, 6, 8):
                            ada_group(l + 1, s // 2, it, 5)

            def head_norm(i, bank):
                dst, gain, T = HN[i]
                dve.wait_ge(sem("hn_root"), i + 1)
                link(dve.reciprocal(HSQ[:, i % 2, 0:T], HSQ[:, i % 2, 0:T]))
                dve.scalar_tensor_tensor(out=dst, in0=PS[:, bank, 0:T], scalar=gain, in1=HSQ[:, i % 2, 0:T],
                                         op0=ALU.mult, op1=ALU.mult).then_inc(sem("hn_done"), 1)

            def attention(a):
                t, n, KC = a["tag"], a["n"], a["kc"]

                def bias(u):
                    h, tt = divmod(u, 2)
                    if u >= 2:
                        dve.wait_ge(sem(f"s_{t}"), u - 1)
                    dve.scalar_tensor_tensor(out=BI[:, u % 2, :], in0=DIST[:, tt, :], scalar=-(2.0 ** -(h + 1)),
                                             in1=SEL[:, tt, :], op0=ALU.mult, op1=ALU.add).then_inc(sem("bias_made"), 1)

                def row_max(u):
                    dve.wait_ge(sem(f"s_{t}"), u + 1)
                    dve.tensor_reduce(NM[:, u % 2:u % 2 + 1], PS[:, u % 2, 0:KC * P], AX.X, ALU.max, negate=True).then_inc(
                        sem(f"max_{t}"), 1)

                def scale(u):
                    dve.wait_ge(sem(f"exp_{t}"), u + 1)
                    link(dve.reciprocal(SM[:, u % 2:u % 2 + 1], SM[:, u % 2:u % 2 + 1]))
                    pb = a["p"][:, u % 2, :]
                    dve.tensor_scalar(pb, pb, SM[:, u % 2:u % 2 + 1], None, ALU.mult).then_inc(sem(f"p_{t}"), 1)

                def out_copy(hp):
                    dve.wait_ge(sem(f"pv_{t}"), 4 * hp + 4)
                    dve.tensor_copy(a["o"][:, hp * SEQ:(hp + 1) * SEQ], PS[:, 4 + hp % 2, 0:SEQ]).then_inc(sem(f"o_{t}"), 1)

                if a["bias"] is not None:
                    bias(0)
                    bias(1)
                row_max(0)
                for u in range(n):
                    if a["bias"] is not None and u + 2 < n:
                        bias(u + 2)
                    scale(u)
                    if u + 1 < n:
                        row_max(u + 1)
                    if u >= 5 and (u - 5) % 4 == 0:
                        out_copy((u - 5) // 4)
                out_copy(n // 4 - 1)

            def dve_gathered():
                slots = NE * CAP
                for t in range(2):
                    pg = PG[:, t, 0:slots].rearrange("p (e s) -> p e s", e=NE)
                    pcw = PCW.rearrange("p (e s) -> p e s", e=NE)
                    iota = IOTA64.unsqueeze(1).to_broadcast([P, NE, CAP])
                    dve.tensor_tensor(pg, iota, RANK[:, t, :].unsqueeze(2).to_broadcast([P, NE, CAP]),
                                      ALU.is_equal).then_inc(sem("place"), 1)
                    dve.memset(PG[:, t, slots:slots + P], 0.0).then_inc(sem("place"), 1)
                    dve.wait_ge(sem("place"), 2 * t + 2)
                    if t:
                        dve.wait_ge(sem("pt_mm"), 4)
                    dve.tensor_tensor(pcw, pg, CMB[:, t, :].unsqueeze(2).to_broadcast([P, NE, CAP]), ALU.mult).then_inc(
                        sem("pcw_made"), 1)
                dve.memset(PTS[:, 0:SEQ], 0.0).then_inc(sem("ys_act"), 1)
                dve.wait_ge(sem("pt_mm"), 8)
                dve.memset(YS, 0.0).then_inc(sem("ys_dve"), 1)
                dve.wait_ge(sem("ys_dve"), 1)
                dve.wait_ge(sem("gathered"), 1)
                dve.tensor_copy(XG[:, 512:1024], PS[:, 1, :]).then_inc(sem("xg_dve"), 1)
                with dve.Fori(0, NE // 2) as it:
                    for e in range(2):
                        dve.wait_ge(sem("m_silu"), it * 2 + (e + 1))
                        dve.tensor_tensor(HF[:, e * 256:(e + 1) * 256].rearrange("p (q s) -> p q s", q=4),
                                          SGF[:, e * 256:(e + 1) * 256].rearrange("p (q s) -> p q s", q=4),
                                          PS[:, e, :].rearrange("p (q g s) -> p q g s", q=4, g=2)[:, :, 1, :],
                                          ALU.mult).then_inc(sem("hf_done"), 1)
                    dve.wait_ge(sem("gathered"), it + 2)
                    dve.tensor_copy(XG[:, 512:1024], PS[:, 1, :]).then_inc(sem("xg_dve"), 1)
                    dve.wait_ge(sem("dn_mm"), it * 2 + 3)
                    dve.wait_ge(sem("scattered"), it + 1)
                    dve.tensor_copy(YS[:, 512:1024], PS[:, 3, :]).then_inc(sem("ys_dve"), 1)
                dve.wait_ge(sem("scattered"), NE // 2 + 1)

            def dve_dense():
                dve.wait_ge(sem("cmb_mm"), 1)
                dve.tensor_copy(CTB, PS[0:NE, 5, 0:SEQ]).then_inc(sem("cmb_copied"), 1)
                dve.wait_ge(sem("cw_copied"), 16)
                with dve.Fori(0, NE // 2) as it:
                    for e in range(2):
                        for q in range(4):
                            dve.wait_ge(sem("m_silu"), it * 8 + (4 * e + q + 1))
                            if q == 0:
                                dve.wait_ge(sem("dn_mm"), it * 2 + 1)
                            sg = SGM[:, q * 256:q * 256 + 256]
                            dve.tensor_tensor(sg, sg, CWB[:, bass.ds((it * 2 + e) * 256, 256)], ALU.mult).then_inc(
                                sem("m_cw"), 1)
                            dve.wait_ge(sem("m_cw"), it * 8 + (4 * e + q + 1))
                            dve.tensor_tensor(HM[:, e * 1024 + q * 256:e * 1024 + q * 256 + 256], sg, PS[:, q, 256:512],
                                              ALU.mult).then_inc(sem("hm_done"), 1)
                dve.wait_ge(sem("dn_mm"), NE + 1)

            for g in range(PE_G, 4):
                if g == 3:
                    norm_root(0)
                ada_group(0, g)
            ada(0, 0, 16, (0,))
            norm(0)
            link(dve.memset(A[:, 9216:9732], 0.0))
            for j in range(KD):
                dve.wait_ge(sem("c_copied"), j + 1)
                if j:
                    dve.wait_ge(sem("conv_done"), j)
                b = 3 * (j % 2)
                w = [vec("conv_w", i * 8 + j, i * 8 + j + 1) for i in range(3)]
                ct = CT[:, (j % 2) * 512:(j % 2) * 512 + 512].rearrange("p (s t) -> p s t", s=2)
                link(dve.tensor_tensor(Z[:, :, 1:257], ct, PS[:, b + 2, :].rearrange("p (s t) -> p s t", s=2), ALU.mult))
                link(dve.tensor_scalar(T1, Z[:, :, 0:256], w[0], None, ALU.mult))
                link(dve.scalar_tensor_tensor(out=T1, in0=Z[:, :, 1:257], scalar=w[1], in1=T1, op0=ALU.mult, op1=ALU.add))
                link(dve.scalar_tensor_tensor(out=T1, in0=Z[:, :, 2:258], scalar=w[2], in1=T1, op0=ALU.mult, op1=ALU.add))
                dve.tensor_tensor(YC[:, j * 512:(j + 1) * 512].rearrange("p (s t) -> p s t", s=2),
                                  PS[:, b, :].rearrange("p (s t) -> p s t", s=2), T1, ALU.mult).then_inc(sem("conv_done"), 1)
                ada_group(0, 4 + j)
            ada(0, 16, 48, (1,))
            residual(0)
            norm(1)
            ffn_in(0)
            residual(1)
            norm(2)
            for i in range(16):
                head_norm(i, i % 3)
            attention(ATT[0])
            residual(2)
            norm(3)
            ffn_in(1)
            residual(3)
            norm(4)
            for i in range(4):
                head_norm(16 + i, i)
            dve.wait_ge(sem("lat_root"), 1)
            link(dve.reciprocal(RN[:, 0:SEQ], RN[:, 0:SEQ]))
            for c in range(2):
                la = LATB[:, c * SEQ:(c + 1) * SEQ]
                dve.scalar_tensor_tensor(out=la, in0=la, scalar=vec("g_lat", c, c + 1), in1=RN[:, 0:SEQ], op0=ALU.mult,
                                         op1=ALU.mult).then_inc(sem("lat_done"), 1)
            for i in range(4):
                head_norm(20 + i, i)
            dve.wait_ge(sem("dist_in"), 16)
            dve.wait_ge(sem("wi_done"), 1)
            link(dve.tensor_scalar(NEGM, DIST, 0.0, NEG, ALU.is_lt, ALU.mult))
            for v in range(16):
                t, h = divmod(v, 8)
                dve.wait_ge(sem("relu"), v + 1)
                prev = NEGM if h == 0 else SCO
                if v:
                    dve.wait_ge(sem("scored"), v)
                dve.scalar_tensor_tensor(out=SCO[:, t, :], in0=RL[:, v % 4, :], scalar=SC3[:, v:v + 1], in1=prev[:, t, :],
                                         op0=ALU.mult, op1=ALU.add).then_inc(sem("scored"), 1)
            dve.wait_ge(sem("scored"), 16)
            for r in range(TOPK // 8):
                dve.max(MX8[:, 0, :], SCO[:, 0, :]).then_inc(sem("top"), 1)
                dve.max(MX8[:, 1, :], SCO[:, 1, :]).then_inc(sem("top"), 1)
                dve.wait_ge(sem("top"), 2 * r + 2)
                link(dve.match_replace(SCO[:, 0, :], MX8[:, 0, :], SCO[:, 0, :], -3e38))
                link(dve.match_replace(SCO[:, 1, :], MX8[:, 1, :], SCO[:, 1, :], -3e38))
            link(dve.tensor_scalar(SEL, SCO, -2e38, NEG, ALU.is_gt, ALU.mult))
            link(dve.tensor_tensor(SEL, SEL, NEGM, ALU.add))
            attention(ATT[1])

            dve.wait_ge(sem("pv_dsa"), 16)
            dve.wait_ge(sem("mixed"), 5)

            for m in range(4):
                sl = slice(m * 256, (m + 1) * 256)
                link(dve.tensor_scalar(KK[:, sl], RK[:, sl], vec("k_k", m, m + 1), None, ALU.mult))
            dve.memset(SC3[:, 32:33], 0.0).then_inc(sem("kk_raw"), 1)
            dve.wait_ge(sem("w_sig"), 4)
            link(dve.tensor_scalar(WW, WW, -float(np.exp(-0.5)), None, ALU.mult))
            dve.wait_ge(sem("reset_in"), 16)
            link(dve.tensor_tensor_scan(LL, RST, WW, 0.0, ALU.mult, ALU.add))
            dve.tensor_tensor(WW, LL, WW, ALU.subtract).then_inc(sem("w_prev"), 1)
            dve.wait_ge(sem("a_sig"), 4)
            dve.wait_ge(sem("kk_root"), 1)
            for m in range(4):
                sl = slice(m * 256, (m + 1) * 256)
                link(dve.tensor_scalar(TS[:, sl], AA[:, sl], -1.0, vec("k_a", m, m + 1), ALU.add, ALU.mult))
                link(dve.scalar_tensor_tensor(out=RK[:, sl], in0=TS[:, sl], scalar=1.0, in1=RK[:, sl], op0=ALU.add,
                                              op1=ALU.mult))
            for m in range(4):
                sl = slice(m * 256, (m + 1) * 256)
                ins = dve.scalar_tensor_tensor(out=EE[:, sl], in0=RR[:, sl], scalar=vec("r_k", m, m + 1), in1=RK[:, sl],
                                               op0=ALU.mult, op1=ALU.mult)
                link(ins)
            dve.memset(SC3[:, 33:34], 0.0).then_inc(sem("rk_made"), 1)
            link(dve.tensor_scalar(RNK, RNK, 1e-12, None, ALU.max))
            link(dve.reciprocal(RNK, RNK))
            link(dve.tensor_tensor(KK, KK, RNK, ALU.mult))
            link(dve.tensor_tensor(BB, KK, AA, ALU.mult))
            dve.wait_ge(sem("rk_sum"), 1)
            dve.wait_ge(sem("w_prev"), 1)
            link(dve.tensor_tensor(BON, ps2(2), RV, ALU.mult))
            dve.memset(SC3[:, 34:35], 0.0).then_inc(sem("cum"), 1)
            dve.wait_ge(sem("exp_prev"), 1)
            link(dve.tensor_tensor(KK, KK, WW, ALU.mult))
            dve.wait_ge(sem("exp_cum"), 1)
            link(dve.tensor_tensor(RR, RR, EE, ALU.mult))
            dve.tensor_copy(DC.rearrange("p (c h) -> p h c", h=HP),
                            EE.rearrange("p (h c t) -> p h c t", h=HP, c=NCH)[:, :, :, CH - 1]).then_inc(sem("used_cum"), 1)
            dve.wait_ge(sem("exp_inv"), 1)
            dve.tensor_tensor(BB, BB, EE, ALU.mult).then_inc(sem("b_hat"), 1)
            dve.tensor_tensor(RK, RK, EE, ALU.mult).then_inc(sem("k_hat"), 1)
            for i, (dst, mask) in enumerate(((ABT, "strict"), (AKT, "strict"), (RBT, "incl"), (RKT, "incl"))):
                b0 = (6, 0, 2, 4)[i]
                dve.wait_ge(sem("tri_mm"), i + 1)
                if i == 0:
                    dve.wait_ge(sem("k_hat"), 1)
                    dve.wait_ge(sem("b_hat"), 1)
                for b in range(2):
                    dve.tensor_tensor(dst[:, b * 512:(b + 1) * 512].rearrange("p (c t) -> p c t", t=64),
                                      PS[:, b0 + b, :].rearrange("p (c t) -> p c t", t=64),
                                      con(mask).unsqueeze(1).to_broadcast([P, 8, 64]), ALU.mult).then_inc(sem("tri_masked"), 1)
            dve.wait_ge(sem("tri_masked"), 8)
            idb = con("id64").unsqueeze(1).to_broadcast([P, 16, 64])
            link(dve.tensor_copy(TI.rearrange("p (c t) -> p c t", t=64), idb))
            link(dve.tensor_copy(TIT.rearrange("p (c t) -> p c t", t=64), idb))
            for lv in range(6):
                if lv:
                    dve.wait_ge(sem("t_done"), 4 * lv)
                dve.tensor_tensor(MX.rearrange("p (c t) -> p c t", t=64), ABT.rearrange("p (c t) -> p c t", t=64),
                                  con("level", lv * 64, lv * 64 + 64).unsqueeze(1).to_broadcast([P, 16, 64]),
                                  ALU.mult).then_inc(sem("lv_masked"), 1)
                for b in range(2):
                    sl = slice(b * 512, (b + 1) * 512)
                    dve.wait_ge(sem("p2_mm"), 2 * lv + b + 1)
                    dve.tensor_tensor(TI[:, sl], TI[:, sl], PS[:, 2 + b, :], ALU.subtract).then_inc(sem("t_done"), 1)
                    dve.tensor_tensor(TIT[:, sl], TIT[:, sl], PS[:, 4 + b, :], ALU.subtract).then_inc(sem("t_done"), 1)
            for c in range(NCH):
                old = ST[:, (c % 2) * 256:(c % 2) * 256 + 256]
                new = ST[:, (1 - c % 2) * 256:(1 - c % 2) * 256 + 256]
                dcb = DC[:, c * HP:(c + 1) * HP].unsqueeze(2).to_broadcast([P, HP, 64])
                n3 = new.rearrange("p (h j) -> p h j", h=HP)
                dve.wait_ge(sem("state_mm"), c + 1)
                if c:
                    dve.wait_ge(sem("y_mm"), c)
                    link(dve.tensor_tensor(new, PS[:, 2, 0:256], old, ALU.add))
                    dve.tensor_tensor(n3, n3, dcb, ALU.mult).then_inc(sem("state"), 1)
                else:
                    dve.tensor_tensor(n3, PS[:, 2, 0:256].rearrange("p (h j) -> p h j", h=HP), dcb, ALU.mult).then_inc(
                        sem("state"), 1)
                dve.wait_ge(sem("state"), c + 1)
            dve.wait_ge(sem("mean_sum"), 1)
            dve.scalar_tensor_tensor(out=YY, in0=ps2(0), scalar=-1.0 / HD, in1=YY, op0=ALU.mult, op1=ALU.add).then_inc(
                sem("centred"), 1)
            dve.wait_ge(sem("var_root"), 1)
            dve.wait_ge(sem("centred"), 1)
            link(dve.reciprocal(TIT, TIT))
            link(dve.tensor_tensor(YY, YY, TIT, ALU.mult))
            for m in range(4):
                sl = slice(m * 256, (m + 1) * 256)
                link(dve.tensor_scalar(YY[:, sl], YY[:, sl], vec("ln_w", m, m + 1), vec("ln_b", m, m + 1), ALU.mult, ALU.add))
            link(dve.tensor_tensor(YY, YY, BON, ALU.add))
            dve.wait_ge(sem("g_copied"), 1)
            dve.tensor_tensor(YY, YY, GG, ALU.mult).then_inc(sem("o_rwkv"), 1)
            for m in range(KD):
                dve.wait_ge(sem("gate_sig"), m + 1)
                if m:
                    dve.wait_ge(sem("merged"), m)
                link(dve.tensor_tensor(TM, SG[:, m % 2, :], PS[:, 2 * (m % 2) + 1, :], ALU.mult))
                dve.tensor_tensor(MG[:, m * SEQ:(m + 1) * SEQ], TM[:, 0:256], TM[:, 256:512], ALU.add).then_inc(
                    sem("merged"), 1)
            residual(4)
            norm(5)
            dve.wait_ge(sem("logits"), 1)
            link(dve.tensor_copy(LG[:, :, 0:36], PS[:, 6, 0:128].rearrange("p (t e) -> p t e", t=2)[:, :, 0:36]))
            G, E = LG[:, :, 0:4], LG[:, :, 4:36]
            link(dve.tensor_tensor(E, E, vec("e_bias").unsqueeze(1).to_broadcast([P, 2, NE]), ALU.add))
            small = RT[:, 8:32]
            gexp = RT[:, 0:8].rearrange("p (t e) -> p t e", t=2)
            oh = [RT[:, 64 + 64 * i:128 + 64 * i].rearrange("p (t e) -> p t e", t=2) for i in range(4)]

            def two(i):
                return small[:, 2 * i:2 * i + 2]

            def wide(i, w):
                return two(i).unsqueeze(2).to_broadcast([P, 2, w])

            def first_max(v, w, m, dst):
                link(dve.tensor_reduce(two(m), v, AX.X, ALU.max))
                link(dve.tensor_tensor(dst, v, wide(m, w), ALU.is_equal))
                link(dve.tensor_scalar(dst, dst, -99.0, 99.0, ALU.mult, ALU.add))
                link(dve.tensor_tensor(dst, dst, con("iota", 0, w).unsqueeze(1).to_broadcast([P, 2, w]), ALU.add))
                link(dve.tensor_reduce(two(11), dst, AX.X, ALU.min))
                link(dve.tensor_tensor(dst, dst, wide(11, w), ALU.is_equal))

            goh = oh[0][:, :, 0:4]
            first_max(G, 4, 1, goh)
            dve.tensor_tensor(gexp, G, wide(1, 4), ALU.subtract).then_inc(sem("g_shift"), 1)
            link(dve.tensor_scalar(goh, goh, -NEG, NEG, ALU.mult, ALU.add))
            link(dve.tensor_tensor(E.rearrange("p t (g e) -> p t g e", g=4), E.rearrange("p t (g e) -> p t g e", g=4),
                                   goh.unsqueeze(3).to_broadcast([P, 2, 4, EPG]), ALU.add))
            first_max(E, NE, 2, oh[1])
            link(dve.scalar_tensor_tensor(out=E, in0=oh[1], scalar=-3e38, in1=E, op0=ALU.mult, op1=ALU.add))
            first_max(E, NE, 3, oh[2])
            dve.tensor_tensor(two(0), two(3), two(2), ALU.subtract).then_inc(sem("e_diff"), 1)
            dve.tensor_tensor(IND, oh[1], oh[2], ALU.add).then_inc(sem("indicated"), 1)
            dve.wait_ge(sem("ranked"), 1)
            dve.scalar_tensor_tensor(out=RANK, in0=PS[:, 6, 0:2 * NE].rearrange("p (t e) -> p t e", t=2), scalar=1.0,
                                     in1=IND, op0=ALU.add, op1=ALU.mult).then_inc(sem("rank_copied"), 1)
            dve.tensor_reduce(FLAG[:, :], PS[:, 6, 2 * NE:3 * NE], AX.X, ALU.max).then_inc(sem("counted"), 1)
            dve.wait_ge(sem("rank_copied"), 1)
            dve.wait_ge(sem("g_exp"), 1)
            link(dve.tensor_reduce(two(4), gexp, AX.X, ALU.add))
            dve.wait_ge(sem("e_exp"), 1)
            link(dve.scalar_tensor_tensor(out=two(5), in0=two(0), scalar=1.0, in1=two(4), op0=ALU.add, op1=ALU.mult))
            link(dve.reciprocal(two(6), two(5)))
            link(dve.tensor_tensor(two(7), two(6), two(0), ALU.mult))
            link(dve.tensor_tensor(oh[1], oh[1], wide(6, NE), ALU.mult))
            link(dve.tensor_tensor(oh[2], oh[2], wide(7, NE), ALU.mult))
            dve.tensor_tensor(CMB, oh[1], oh[2], ALU.add).then_inc(sem("combined"), 1)
            dve.memset(CT0, 0.0).then_inc(sem("zeros"), 1)
            dve.wait_ge(sem("combined"), 1)
            busiest = count_of(dve)
            with dve.If(busiest < CAP + 1):
                dve_gathered()
            with dve.Else():
                dve_dense()
            for m in range(KD):
                xs = X[:, m * SEQ:(m + 1) * SEQ]
                dve.scalar_tensor_tensor(out=xs, in0=PS[:, 4 + m // 2, (m % 2) * 256:(m % 2) * 256 + 256],
                                         scalar=mod(2, 40 + m, 1), in1=xs, op0=ALU.mult, op1=ALU.add).then_inc(
                    sem("y_out"), 1)


def feature_major(a):
    t, f = a.shape
    return a.T.reshape(f // P, P, t).transpose(1, 0, 2).reshape(P, -1)


def columns(v):
    return v.reshape(-1, P).T


def tiles(w, per_slot):
    k, m = w.shape
    return w.reshape(k // P, P, m // (per_slot * P), per_slot * P).transpose(2, 1, 0, 3).reshape(
        m // (per_slot * P), P, -1)


def chunks_in_order(w, order):
    k, m = w.shape
    return w.reshape(k, m // P, P)[:, order].reshape(k, -1)


def host_consts():
    c = np.zeros((P, NCONST), np.float32)
    i = np.arange(P)
    r, t = i[:, None] % 64, np.arange(64)[None, :]

    def put(name, a):
        c[:, COFF[name]:COFF[name] + a.shape[1]] = a

    put("ident", np.eye(P))
    put("ones", np.ones((P, P)))
    put("bo64", (i[:, None] // 64 == i[None, :] // 64) * 1.0)
    put("id64", (r == t) * 1.0)
    put("strict", (r < t) * 1.0)
    put("incl", (r <= t) * 1.0)
    lv = []
    for n in range(6):
        b = 1 << n
        lv.append((r // (2 * b) == t // (2 * b)) & (r % (2 * b) < b) & (t % (2 * b) >= b))
    put("level", np.concatenate(lv, 1) * 1.0)
    put("iota", np.broadcast_to(np.arange(32.0), (P, 32)))
    put("eps", np.broadcast_to(np.array([EPS, GN_EPS, EPS * HD]), (P, 3)))
    q = np.arange(P)[:, None] % GRID_W
    k = np.arange(GRID_W)[None, :]
    start = np.clip(q - NA_COLS // 2, 0, GRID_W - NA_COLS)
    colmask = np.where((k >= start) & (k < start + NA_COLS), 0.0, NEG).astype(np.float32)
    tok = np.arange(SEQ)
    dist = np.concatenate([np.arange(P)[:, None] + P * t2 - tok[None, :] for t2 in range(2)], 1).astype(np.float32)
    reset = np.broadcast_to((np.arange(HP * SEQ) % CH != 0).astype(np.float32), (P, HP * SEQ)).copy()
    return c, colmask, dist, reset


def kernel(**inp):
    import concourse.bacc as bacc
    from concourse.bass_utils import run_bass_kernel_spmd

    a = {k: np.asarray(v) for k, v in inp.items()}
    cat = np.concatenate

    shift_w = 1824
    r_w = 512
    mu = a["rwkv_mu_2"][0]

    def shift_cols(w, axis):
        r_, k_, v_, wl, al, gl = np.split(w, [512, 1024, 1536, 1600, 1664], axis=axis)
        pad = np.zeros(w.shape[:axis] + (96,) + w.shape[axis + 1:], w.dtype)
        return cat([wl, al, gl, pad, r_, k_, v_], axis=axis)

    two = lambda g: np.concatenate([g, g])[:, None]
    router = cat([a["router_group_w_2"][0], a["router_expert_w_2"][0]], 1)
    w_in = a["w_in_2"][0]
    q_a, kv, q_i, k_i, w_i, shf, g_a, g_r = np.split(w_in, np.cumsum([512, 256, 256, 32, 8, shift_w, 1024]), axis=1)
    cs = np.stack([columns(a["c"][0]), columns(a["c_ctx"]), columns(a["c_2"][0])], 2).reshape(P, 24)
    parts = {
        "b_ada": cat([columns(a["b_ada"][0]), columns(a["b_ada"][1]), columns(a["ada_b_2"][0])], 1),
        "g_norm": cat([columns(v) for v in (a["norm_mix"][0], a["norm_ffn"][0], a["norm_mix"][1], a["norm_ffn"][1],
                                            a["mix_norm_g_2"][0], a["moe_norm_g_2"][0])], 1),
        "conv_w": cat([columns(a["conv_w"][0, i]) for i in range(3)], 1),
        "qk1": cat([two(a["attn_q_norm"][0]), two(a["attn_k_norm"][0])], 1),
        "qk2": cat([two(a["q_norm_g_2"][0]), two(a["k_norm_g_2"][0])], 1),
        "g_lat": columns(a["kv_norm_g_2"][0]),
        "mu": columns(shift_cols(mu, 0)),
        "w0": columns(a["rwkv_w0_2"][0]), "a0": columns(a["rwkv_a0_2"][0]), "k_k": columns(a["rwkv_k_k_2"][0]),
        "k_a": columns(a["rwkv_k_a_2"][0]), "r_k": columns(a["rwkv_r_k_2"][0].reshape(-1)),
        "ln_w": columns(a["rwkv_ln_w_2"][0]), "ln_b": columns(a["rwkv_ln_b_2"][0]),
        "cs": cs,
        "e_bias": np.broadcast_to(a["router_expert_bias_2"][0][None], (P, NE)),
        "w_i": tiles_small(w_i), "router": tiles_small(router),
    }
    vecs = cat([parts[n] for n, _ in VECS], 1)

    conv_order = [x for j in range(8) for x in (j, 8 + j, 16 + j)]
    gu_order = [x for j in range(KF) for x in (j, KF + j)]
    wi = cat([kv, q_i, q_a, k_i, k_i, k_i, k_i, shift_cols(shf, 1)], 1)
    qkv = a["attn_w_qkv"][0]
    lora = cat([cat([a["rwkv_w2_2"][0], a["rwkv_a2_2"][0]], 0), a["rwkv_g2_2"][0][:128],
                cat([a["rwkv_g2_2"][0][128:], np.zeros((96, 512), np.float32)], 0)], 1)[None]
    ga, gr, ba, br = (tiles(w, 1) for w in (g_a, g_r, a["w_branch_attn_2"][0], a["w_branch_rwkv_2"][0]))
    wg, wu, wd = a["expert_w_gate_2"][0], a["expert_w_up_2"][0], a["expert_w_down_2"][0]
    gu = np.stack([wg.reshape(NE, KD, P, 4, P), wu.reshape(NE, KD, P, 4, P)], 4)
    gu = gu.reshape(NE, KD, P, 2, 2, 2, P).transpose(0, 3, 2, 1, 4, 5, 6).reshape(NE, 2, P, 4096)
    dn = wd.reshape(NE, 4, P, D).transpose(0, 2, 1, 3).reshape(NE, 1, P, 4096)
    W = {
        "ada0": tiles(a["w_ada"][0], 4)[:PE_G],
        "conv": tiles(chunks_in_order(a["conv_w_in"][0], conv_order), 3), "cout": tiles(a["conv_w_out"][0], 4),
        "fin0": tiles(chunks_in_order(a["ffn_w_in"][0], gu_order), 2), "fout0": tiles(a["ffn_w_out"][0], 1),
        "fin1": tiles(chunks_in_order(a["ffn_w_in"][1], gu_order), 2), "fout1": tiles(a["ffn_w_out"][1], 1),
        "qkv": tiles(qkv, 4), "aout": tiles(a["attn_w_out"][0], 4),
        "win": tiles(wi, 4), "kvup": tiles(a["w_kv_up_2"][0], 8), "lora": lora,
        "gates": cat([ga, gr, ba, br], 2), "wout": tiles(a["w_out_2"][0], 4),
        "moe": cat([gu.reshape(NE // 2, 4, P, 4096), dn.reshape(NE // 2, 2, P, 4096)], 1).reshape(NE * 3, P, 4096),
    }
    ada = cat([tiles(a["w_ada"][0], 4)[PE_G:], tiles(a["w_ada"][1], 4), tiles(a["ada_w_2"][0], 4)], 0)
    ada = ada.reshape(-1, P, PARTS, 2 * GRP).transpose(0, 2, 1, 3).reshape(-1, P, 2 * GRP)
    rp = np.stack([a["attn_rpb"][0][:, 5:11, :], a["attn_rpb"][0][:, 4:10, :]])
    pad = (GRID_W - 1) - (NA_COLS - 1)
    rp = np.pad(rp, ((0, 0), (0, 0), (0, 0), (pad, pad)))
    c, colmask, dist, reset = host_consts()
    rank_c = cat([np.triu(np.ones((P, P), np.float32), 1), np.broadcast_to(np.arange(1.0, CAP + 1.0, dtype=np.float32), (P, CAP))], 1)
    xin = cat([feature_major(a["x"][0]), feature_major(a["ctx"][0])], 1)

    nc = bacc.Bacc("TRN2", target_bir_lowering=False, num_devices=1)
    arrays, aps = {}, {}

    def give(name, arr):
        arr = np.ascontiguousarray(arr)
        arrays[name] = arr
        aps[name] = nc.dram_tensor(name, arr.shape, F32, kind="ExternalInput").ap()
        return aps[name]

    Wap = {k: give(f"w_{k}", v) for k, v in W.items()}
    out = nc.dram_tensor("out", (P, 2048), F32, kind="ExternalOutput").ap()
    slide = np.arange(GRID_W)[None, :] - np.arange(GRID_W)[:, None] + GRID_W - 1
    table = rp[:, :, :, slide].transpose(0, 3, 1, 2, 4).reshape(P, -1)
    build(nc, give("xin", xin), give("ada", ada), give("vecs", vecs), give("consts", c), give("colmask", colmask), give("dist", dist),
          give("reset", reset), give("rpb", table),
          give("rank_c", rank_c), Wap, out)
    r = run_bass_kernel_spmd(nc, [arrays], core_ids=[0])
    y = r.results[0]["out"]
    return y.reshape(P, KD, SEQ).transpose(2, 1, 0).reshape(1, SEQ, D)


def tiles_small(w):
    return w.reshape(KD, P, -1).transpose(1, 0, 2).reshape(P, -1)
```
